# Optimizing a Trainium2 kernel written in Bass

```python
import jax, jax.numpy as jnp
from jax import lax
import numpy as np

D_MODEL = 1024
BATCH = 1
SEQ = 2048
DEPTH = 1

CHUNK = 64
N_MIXERS = 4
HEAD_DIM = 64
N_HEADS = D_MODEL // HEAD_DIM
MIX_WIDTH = N_HEADS * HEAD_DIM
A_KV_HEADS = 2
A_WINDOW = 128
A_WINDOW_CHUNKS = A_WINDOW // CHUNK
B_QBLOCK = 128
C_KERNEL = 31
C_CHANNELS = MIX_WIDTH
D_PREV_CHUNKS = 8
D_BAND = D_PREV_CHUNKS + 1
D_MAX_REL = 128
D_REL_SIZE = (CHUNK - 1) + D_MAX_REL + 1
N_MEM = 256
MEM_HEADS = 4
MEM_WIDTH = MEM_HEADS * HEAD_DIM
BRANCH_WIDTH = MIX_WIDTH + MEM_WIDTH
EPS = 1e-6
NEG = -1e30

A_IN = N_HEADS * HEAD_DIM + 2 * A_KV_HEADS * HEAD_DIM
B_IN = 3 * MIX_WIDTH + N_HEADS
C_IN = 2 * C_CHANNELS
D_IN = 3 * MIX_WIDTH
MIXER_IN = (A_IN, B_IN, C_IN, D_IN)

kernel_name = 'hybrid_streaming_encoder_block'

def rms_norm(x, g):
    xf = x.astype(jnp.float32)
    y = xf * lax.rsqrt(jnp.mean(xf * xf, axis=-1, keepdims=True) + EPS)
    return (y * g.astype(jnp.float32)).astype(x.dtype)

def alibi_slopes(n_heads):
    return 2.0 ** (-8.0 * jnp.arange(1, n_heads + 1, dtype=jnp.float32) / n_heads)

def sliding_window_sink_attention(u, qn_g, kn_g, sink):
    B, S, _ = u.shape
    NC = S // CHUNK
    G = N_HEADS // A_KV_HEADS
    W = A_WINDOW_CHUNKS
    f32 = jnp.float32
    q, k, v = jnp.split(u, [N_HEADS * HEAD_DIM, N_HEADS * HEAD_DIM + A_KV_HEADS * HEAD_DIM], axis=-1)
    q = rms_norm(q.reshape(B, S, N_HEADS, HEAD_DIM), qn_g).astype(f32).reshape(B, NC, CHUNK, A_KV_HEADS, G, HEAD_DIM)
    k = rms_norm(k.reshape(B, S, A_KV_HEADS, HEAD_DIM), kn_g).astype(f32).reshape(B, NC, CHUNK, A_KV_HEADS, HEAD_DIM)
    v = v.astype(f32).reshape(B, NC, CHUNK, A_KV_HEADS, HEAD_DIM)
    pad = ((0, 0), (W - 1, 0), (0, 0), (0, 0), (0, 0))
    kp = jnp.pad(k, pad)
    vp = jnp.pad(v, pad)
    kb = jnp.concatenate([kp[:, o:o + NC] for o in range(W)], axis=2)
    vb = jnp.concatenate([vp[:, o:o + NC] for o in range(W)], axis=2)
    logits = jnp.einsum('bnqkgd,bnskd->bnkgqs', q, kb) * HEAD_DIM ** -0.5
    i = jnp.arange(CHUNK)[:, None]
    j = jnp.arange(W * CHUNK)[None, :]
    dist = jnp.abs(i - j + (W - 1) * CHUNK).astype(f32)
    slopes = alibi_slopes(N_HEADS).reshape(A_KV_HEADS, G)
    logits = logits - slopes[:, :, None, None] * dist
    key_chunk = jnp.arange(NC)[:, None] - (W - 1) + jnp.arange(W * CHUNK)[None, :] // CHUNK
    valid = key_chunk >= 0
    logits = jnp.where(valid[None, :, None, None, None, :], logits, NEG)
    sink_f = sink.astype(f32).reshape(A_KV_HEADS, G)[None, None, :, :, None, None]
    m = jnp.maximum(jnp.max(logits, axis=-1, keepdims=True), sink_f)
    p = jnp.exp(logits - m)
    p = p / (jnp.sum(p, axis=-1, keepdims=True) + jnp.exp(sink_f - m))
    out = jnp.einsum('bnkgqs,bnskd->bnqkgd', p, vb)
    return out.reshape(B, S, MIX_WIDTH)

def forgetting_attention(u, f_bias, qn_g, kn_g):
    B, S, _ = u.shape
    f32 = jnp.float32
    q, k, v, f = jnp.split(u, [MIX_WIDTH, 2 * MIX_WIDTH, 3 * MIX_WIDTH], axis=-1)
    q = rms_norm(q.reshape(B, S, N_HEADS, HEAD_DIM), qn_g).astype(f32)
    k = rms_norm(k.reshape(B, S, N_HEADS, HEAD_DIM), kn_g).astype(f32)
    v = v.astype(f32).reshape(B, S, N_HEADS, HEAD_DIM)
    log_f = jax.nn.log_sigmoid(f.astype(f32) + f_bias.astype(f32))
    F = jnp.cumsum(log_f, axis=1)
    Ft = F.transpose(0, 2, 1)
    NQB = S // B_QBLOCK
    qb = q.reshape(B, NQB, B_QBLOCK, N_HEADS, HEAD_DIM).transpose(1, 0, 2, 3, 4)
    Fb = F.reshape(B, NQB, B_QBLOCK, N_HEADS).transpose(1, 0, 3, 2)
    pos = jnp.arange(S)
    scale = HEAD_DIM ** -0.5

    def block(args):
        q_blk, F_q, n = args
        t = n * B_QBLOCK + jnp.arange(B_QBLOCK)
        logits = jnp.einsum('bqhd,bshd->bhqs', q_blk, k) * scale
        logits = logits + F_q[..., None] - Ft[:, :, None, :]
        logits = jnp.where(pos[None, :] <= t[:, None], logits, NEG)
        p = jax.nn.softmax(logits, axis=-1)
        return jnp.einsum('bhqs,bshd->bqhd', p, v)

    out = lax.map(block, (qb, Fb, jnp.arange(NQB)))
    return out.transpose(1, 0, 2, 3, 4).reshape(B, S, MIX_WIDTH)

def conformer_conv(u, pw_b, dw_w, dw_b, ln_g, ln_b):
    a, g = jnp.split(u + pw_b, 2, axis=-1)
    h = a * jax.nn.sigmoid(g)
    h = lax.conv_general_dilated(
        h, dw_w[:, None, :].astype(h.dtype), window_strides=(1,),
        padding=[(C_KERNEL - 1, 0)], dimension_numbers=('NWC', 'WIO', 'NWC'),
        feature_group_count=C_CHANNELS) + dw_b
    hf = h.astype(jnp.float32)
    mu = jnp.mean(hf, axis=-1, keepdims=True)
    var = jnp.mean(jnp.square(hf - mu), axis=-1, keepdims=True)
    hn = (hf - mu) * lax.rsqrt(var + EPS) * ln_g.astype(jnp.float32) + ln_b.astype(jnp.float32)
    return jax.nn.silu(hn).astype(u.dtype)

def chunk_relpos_attention(u, qn_g, kn_g, rel_tab):
    B, S, _ = u.shape
    NC = S // CHUNK
    P = D_PREV_CHUNKS
    f32 = jnp.float32
    q, k, v = jnp.split(u, [MIX_WIDTH, 2 * MIX_WIDTH], axis=-1)
    q = rms_norm(q.reshape(B, S, N_HEADS, HEAD_DIM), qn_g).astype(f32).reshape(B, NC, CHUNK, N_HEADS, HEAD_DIM)
    k = rms_norm(k.reshape(B, S, N_HEADS, HEAD_DIM), kn_g).astype(f32).reshape(B, NC, CHUNK, N_HEADS, HEAD_DIM)
    v = v.astype(f32).reshape(B, NC, CHUNK, N_HEADS, HEAD_DIM)
    pad = ((0, 0), (P, 0), (0, 0), (0, 0), (0, 0))
    kp = jnp.pad(k, pad)
    vp = jnp.pad(v, pad)
    i = jnp.arange(CHUNK)[:, None]
    j = jnp.arange(D_BAND * CHUNK)[None, :]
    rel = i - j + P * CHUNK
    idx = jnp.clip(rel, -(CHUNK - 1), D_MAX_REL) + (CHUNK - 1)
    bias = rel_tab.astype(f32)[:, idx]
    scale = HEAD_DIM ** -0.5

    def block(args):
        q_c, c = args
        kb = lax.dynamic_slice_in_dim(kp, c, D_BAND, axis=1).reshape(B, D_BAND * CHUNK, N_HEADS, HEAD_DIM)
        vb = lax.dynamic_slice_in_dim(vp, c, D_BAND, axis=1).reshape(B, D_BAND * CHUNK, N_HEADS, HEAD_DIM)
        logits = jnp.einsum('bqhd,bshd->bhqs', q_c, kb) * scale + bias
        valid = (c - P + jnp.arange(D_BAND * CHUNK) // CHUNK) >= 0
        logits = jnp.where(valid, logits, NEG)
        p = jax.nn.softmax(logits, axis=-1)
        return jnp.einsum('bhqs,bshd->bqhd', p, vb)

    out = lax.map(block, (q.transpose(1, 0, 2, 3, 4), jnp.arange(NC)))
    return out.transpose(1, 0, 2, 3, 4).reshape(B, S, MIX_WIDTH)

def memory_cross_attention(uq, qn_g, mem_k, mem_v):
    B, S, _ = uq.shape
    q = rms_norm(uq.reshape(B, S, MEM_HEADS, HEAD_DIM), qn_g).astype(jnp.float32)
    logits = jnp.einsum('bshd,bmhd->bhsm', q, mem_k) * HEAD_DIM ** -0.5
    p = jax.nn.softmax(logits, axis=-1)
    return jnp.einsum('bhsm,bmhd->bshd', p, mem_v).reshape(B, S, MEM_WIDTH)

def setup_inputs(seed: int = 0) -> dict:
    key = jax.random.key(seed)
    ks = jax.random.split(key, 26)
    f32 = jnp.float32

    def nrm(k, shape, scale):
        return jax.random.normal(k, shape, f32) * scale

    def gain(k, shape):
        return 1.0 + 0.1 * jax.random.normal(k, shape, f32)

    nA, nB, nC, nD = (len(range(m, DEPTH, N_MIXERS)) for m in range(N_MIXERS))

    def cols(m):
        return MIXER_IN[m] + MEM_WIDTH + BRANCH_WIDTH

    return {
        'x': nrm(ks[0], (BATCH, SEQ, D_MODEL), 1.0),
        'mem': nrm(ks[1], (BATCH, N_MEM, D_MODEL), 1.0),
        'norm_g': gain(ks[2], (DEPTH, D_MODEL)),
        'mem_q_norm_g': gain(ks[3], (DEPTH, HEAD_DIM)),
        'w_out': nrm(ks[4], (DEPTH, BRANCH_WIDTH, D_MODEL), BRANCH_WIDTH ** -0.5),
        'a_w_in': nrm(ks[5], (nA, D_MODEL, cols(0)), D_MODEL ** -0.5),
        'a_q_norm_g': gain(ks[6], (nA, HEAD_DIM)),
        'a_k_norm_g': gain(ks[7], (nA, HEAD_DIM)),
        'a_sink': nrm(ks[8], (nA, N_HEADS), 0.5),
        'b_w_in': nrm(ks[9], (nB, D_MODEL, cols(1)), D_MODEL ** -0.5),
        'b_f_bias': 1.0 + 0.5 * jax.random.normal(ks[10], (nB, N_HEADS), f32),
        'b_q_norm_g': gain(ks[11], (nB, HEAD_DIM)),
        'b_k_norm_g': gain(ks[12], (nB, HEAD_DIM)),
        'c_w_in': nrm(ks[13], (nC, D_MODEL, cols(2)), D_MODEL ** -0.5),
        'c_pw_bias': nrm(ks[14], (nC, 2 * C_CHANNELS), 0.02),
        'c_dw_w': nrm(ks[15], (nC, C_KERNEL, C_CHANNELS), C_KERNEL ** -0.5),
        'c_dw_bias': nrm(ks[16], (nC, C_CHANNELS), 0.02),
        'c_ln_g': gain(ks[17], (nC, C_CHANNELS)),
        'c_ln_b': nrm(ks[18], (nC, C_CHANNELS), 0.02),
        'd_w_in': nrm(ks[19], (nD, D_MODEL, cols(3)), D_MODEL ** -0.5),
        'd_q_norm_g': gain(ks[20], (nD, HEAD_DIM)),
        'd_k_norm_g': gain(ks[21], (nD, HEAD_DIM)),
        'd_rel_bias': nrm(ks[22], (nD, N_HEADS, D_REL_SIZE), 0.5),
        'mem_norm_g': gain(ks[23], (D_MODEL,)),
        'mem_w_kv': nrm(ks[24], (D_MODEL, 2 * MEM_WIDTH), D_MODEL ** -0.5),
        'mem_k_norm_g': gain(ks[25], (HEAD_DIM,)),
    }

def reference(x, mem, norm_g, mem_q_norm_g, w_out,
              a_w_in, a_q_norm_g, a_k_norm_g, a_sink,
              b_w_in, b_f_bias, b_q_norm_g, b_k_norm_g,
              c_w_in, c_pw_bias, c_dw_w, c_dw_bias, c_ln_g, c_ln_b,
              d_w_in, d_q_norm_g, d_k_norm_g, d_rel_bias,
              mem_norm_g, mem_w_kv, mem_k_norm_g):
    B = x.shape[0]
    mk, mv = jnp.split(rms_norm(mem, mem_norm_g) @ mem_w_kv, 2, axis=-1)
    mk = rms_norm(mk.reshape(B, -1, MEM_HEADS, HEAD_DIM), mem_k_norm_g).astype(jnp.float32)
    mv = mv.reshape(B, -1, MEM_HEADS, HEAD_DIM).astype(jnp.float32)
    w_in = (a_w_in, b_w_in, c_w_in, d_w_in)
    for i in range(DEPTH):
        kind, j = i % N_MIXERS, i // N_MIXERS
        u = rms_norm(x, norm_g[i]) @ w_in[kind][j]
        u_mix, u_memq, u_gate = jnp.split(u, [MIXER_IN[kind], MIXER_IN[kind] + MEM_WIDTH], axis=-1)
        if kind == 0:
            y_mix = sliding_window_sink_attention(u_mix, a_q_norm_g[j], a_k_norm_g[j], a_sink[j])
        elif kind == 1:
            y_mix = forgetting_attention(u_mix, b_f_bias[j], b_q_norm_g[j], b_k_norm_g[j])
        elif kind == 2:
            y_mix = conformer_conv(u_mix, c_pw_bias[j], c_dw_w[j], c_dw_bias[j], c_ln_g[j], c_ln_b[j])
        else:
            y_mix = chunk_relpos_attention(u_mix, d_q_norm_g[j], d_k_norm_g[j], d_rel_bias[j])
        y_mem = memory_cross_attention(u_memq, mem_q_norm_g[i], mk, mv)
        y = jnp.concatenate([y_mix.astype(x.dtype), y_mem.astype(x.dtype)], axis=-1) * jax.nn.silu(u_gate)
        x = x + y @ w_out[i]
    return x


_drawn_inputs = setup_inputs


def setup_inputs(seed=0):
    import zlib

    import numpy as np

    out = dict(_drawn_inputs(seed))
    spreads = {}
    factors = {'mem_q_norm_g': 8.0,
     'a_q_norm_g': 4.417,
     'a_k_norm_g': 4.775,
     'a_sink': 64.0,
     'mem_norm_g': 8.0,
     'mem_k_norm_g': 8.0}
    for name, (base, spread) in spreads.items():
        noise = np.random.default_rng([zlib.crc32(name.encode()), seed]).standard_normal(out[name].shape)
        drawn = base * np.exp(spread * noise) if base else spread * noise
        out[name] = __import__('jax').numpy.asarray(drawn.astype(out[name].dtype))
    for name, factor in factors.items():
        out[name] = (out[name] * factor).astype(out[name].dtype)
    return out
```

```python
from contextlib import ExitStack

import concourse.bass as bass
from concourse import mybir

F32 = mybir.dt.float32
F32R = mybir.dt.float32r
BF16 = mybir.dt.bfloat16
ALU = mybir.AluOpType
ACT = mybir.ActivationFunctionType
AX = mybir.AxisListType

P = 128
D_MODEL, SEQ, N_MEM = 1024, 2048, 256
HD = 64
CHUNK = 64
N_HEADS, KV_HEADS, MEM_HEADS = 16, 2, 4
EPS = 1e-6
BLOCK = 512
BLOCKS = SEQ // BLOCK
TILES = BLOCK // P
KT = D_MODEL // P
YT = (N_HEADS + MEM_HEADS) // 2
PAIRS = N_HEADS // 2
CPB = BLOCK // CHUNK
BIG = 3.0e38

A_KV, A_Q0, A_Q1 = 0, 8, 16
G_0, G_1, G_2 = 24, 28, 36
O_0, O_1 = 44, 54
STEPS = 64
LEAD = 3
WRING = 4
UNITS = STEPS // 2
A_ENDS = (7, 15, 23)
G_ENDS = {27: (0, 2), 35: (2, 4), 43: (6, 4)}
O_ENDS = {53: 0, 63: 1}
PRO_CHUNKS = KT

MEM_UNITS = 8
WIN_UNITS = 16
N_UNITS = MEM_UNITS + WIN_UNITS
SLOT = {}
for i in range(MEM_UNITS + 3):
    SLOT.setdefault(12 + i, []).append((0, MEM_UNITS, i))
for i in range(WIN_UNITS + 3):
    SLOT.setdefault(27 + i, []).append((MEM_UNITS, WIN_UNITS, i))


def stage(n, lag):
    return [first + i - lag for first, count, i in SLOT.get(n, []) if 0 <= i - lag < count]


TP_AT = {}
for s, e in enumerate(A_ENDS):
    for t in range(TILES):
        TP_AT[(e + 3 + t // 2, 0 if t % 2 == 0 else 2)] = ("q", s, t)
for n in range(STEPS):
    for u in stage(n, 2):
        TP_AT[(n, 1)] = ("p", u, 0)
X_AT = {47: (0, 0), 48: (0, 1), 51: (1, 0), 52: (1, 1), 55: (2, 0), 56: (2, 1), 59: (3, 0), 60: (3, 1)}
for n, (t, h) in X_AT.items():
    TP_AT[(n, 1)] = ("x", t, h)
TP_ORDER = sorted(TP_AT)
TP_INDEX = {key: i for i, key in enumerate(TP_ORDER)}
TP_HI = {}
for key in TP_ORDER:
    if TP_AT[key][0] != "q":
        TP_HI[key] = len(TP_HI)
PRO_TP = 14
PRO_TP_HI = 12
FINALS = (*A_ENDS, *G_ENDS, *O_ENDS)
X_SQUARE = {45: 0, 49: 1, 53: 2, 57: 3}
Y_GATE = {41: 0, 42: 1, **{43 + k: k for k in range(2, YT)}}
X_SCALE = {46: 0, 50: 1, 54: 2, 58: 3}


def banks(n):
    return sum(2 if e == 27 else 4 for e in FINALS if e <= n)


def bank_free(n, t):
    return {A_KV: ("o_done", t - 3), A_Q0: ("u_raw", t + 1), A_Q1: ("u_raw", 4 + t + 1), G_0: ("u_raw", 8 + t + 1),
            G_1: ("g_done", t + 1) if t < 2 else ("u_raw", 8 + t + 1), G_2: ("g_done", 2 + t + 1),
            O_0: ("g_done", 6 + t + 1), O_1: ("o_done", t + 1)}[n]


class Count:
    def __init__(self, sem, per, base):
        self.sem, self.per, self.base = sem, per, base

    def at(self, turn, n):
        return turn * self.per + (self.base + n)


def encoder_layer(nc, x, mem, w_in, w_gate0, w_out, w_kv, norm_g, mem_norm_g, gains, sink, ident_d, alibi, out):
    ctx = ExitStack()
    with ctx:
        def sb(name, shape, dt=F32):
            return ctx.enter_context(nc.sbuf_tensor(name, shape, dt))

        def count(name, per, base):
            return Count(ctx.enter_context(nc.semaphore(name)), per, base)

        raw = sb("raw", [P, 2, 1024])
        ws = sb("w_split", [P, WRING, 2, 512], F32R)
        xnT = sb("xnT", [P, 2, KT, BLOCK], F32R)
        xt = sb("xt", [P, 2, D_MODEL])
        junk = sb("junk", [P, D_MODEL], BF16)
        gx = sb("gx", [P, D_MODEL])
        u_tok = sb("u_tok", [P, TILES, 512])
        usq = sb("usq", [P, 512])
        qT = sb("qT", [P, CPB, 8, CHUNK])
        mqT = sb("mqT", [P, 2, BLOCK])
        kTo = sb("kT_odd", [P, TILES, P])
        kTe = sb("kT_even", [P, TILES + 1, 2, CHUNK])
        vO = sb("v_odd", [P, TILES, 2, P], F32R)
        vE = sb("v_even", [P, TILES + 1, 2, P], F32R)
        mkT = sb("mkT", [P, 2, N_MEM])
        mv = sb("mv", [P, 2, 2, 256], F32R)
        ps = sb("p_score", [P, 3, 512])
        pT = sb("pT", [P, 2, 2, 512], F32R)
        y = sb("y", [P, YT, BLOCK])
        gate = sb("gate", [P, YT, BLOCK])
        ys = sb("y_split", [P, 2, 2, BLOCK], F32R)
        res = sb("res", [P, TILES, 512])
        bias = sb("alibi_sb", [P, 3, PAIRS, P])
        ident = sb("ident", [P, P])
        zeros = sb("zeros", [P, 256])
        gn = sb("gn", [P, 4])
        snk = sb("snk", [P, PAIRS])
        nsnk = sb("nsnk", [P, PAIRS])
        half = sb("half", [P, 8])
        xss = sb("xss", [P, 2])
        xvar = sb("xvar", [P, 2])
        xr = sb("xr", [P, 2])
        uss = sb("uss", [P, TILES, 8])
        uvar = sb("uvar", [P, TILES, 8])
        ur = sb("ur", [P, TILES, 8])
        nmax = sb("nmax", [P, 3, 4])
        dsk = sb("dsk", [P, 3, 4])
        esk = sb("esk", [P, 3, 4])
        den = sb("den", [P, 3, 4])
        dtot = sb("dtot", [P, 3, 4])
        rinv = sb("rinv", [P, 3, 4])

        acc = [ctx.enter_context(nc.psum_tensor(f"acc{i}", [P, 512], F32)) for i in range(TILES)]
        tp = ctx.enter_context(nc.psum_tensor("tp", [P, 512], F32))
        sc = [ctx.enter_context(nc.psum_tensor(f"sc{i}", [P, 512], F32)) for i in range(2)]
        yb = ctx.enter_context(nc.psum_tensor("yb", [P, 512], F32))

        raw_full = [count(f"raw_full{i}", 16 * UNITS // 2, 32) for i in range(2)]
        w_hi = count("w_hi", STEPS, PRO_CHUNKS)
        w_lo = count("w_lo", STEPS, PRO_CHUNKS)
        step_done = count("step_done", STEPS - len(FINALS), PRO_CHUNKS - 1)
        acc_done = count("acc_done", 30, 2)
        x_full = [count(f"x_full{i}", 32, 48) for i in range(2)]
        x_sq = count("x_sq", 4, 6)
        x_var = count("x_var", 4, 6)
        x_r = count("x_r", 4, 6)
        x_n = count("x_n", 4, 6)
        u_raw = count("u_raw", 12, 2)
        u_sq = count("u_sq", 12, 2)
        u_ss = count("u_ss", 12, 2)
        u_var = count("u_var", 12, 2)
        u_r = count("u_r", 12, 2)
        u_n = count("u_n", 12, 2)
        v_hi = count("v_hi", 4, 2)
        v_lo = count("v_lo", 4, 2)
        v_even = count("v_even", 4, 0)
        halo = count("halo", 1, 1)
        tp_full = count("tp_full", len(TP_ORDER), PRO_TP)
        tp_hi = count("tp_hi", len(TP_HI), PRO_TP_HI)
        tp_free = count("tp_free", len(TP_ORDER), PRO_TP)
        sc_full = count("sc_full", N_UNITS, 0)
        sc_neg = count("sc_neg", N_UNITS, 0)
        sk_arg = count("sk_arg", WIN_UNITS, 0)
        p_exp = count("p_exp", N_UNITS, 0)
        d_sum = count("d_sum", WIN_UNITS, 0)
        p_rinv = count("p_rinv", N_UNITS, 0)
        p_norm = count("p_norm", N_UNITS, 0)
        y_full = count("y_full", N_UNITS, 0)
        y_free = count("y_free", N_UNITS, 0)
        g_th = count("g_th", YT, 0)
        g_done = count("g_done", YT, 0)
        y_prod = count("y_prod", YT, 0)
        y_hi = count("y_hi", 2 * YT, 0)
        y_lo = count("y_lo", 2 * YT, 0)
        res_full = count("res_full", 32, 0)
        o_done = count("o_done", 8, 4)
        stored = count("stored", 128, 64)
        const = count("const", 0, 0)
        ready = count("ready", 0, 0)
        N_CONST = 16 * 8

        def step_over(b, n):
            if n in FINALS or n == -1:
                return acc_done, acc_done.at(b, banks(n))
            return step_done, step_done.at(b, sum(m not in FINALS for m in range(n + 1)))

        block = ctx.enter_context(nc.Block())

        def w_unit(u):
            if u < 12:
                return w_in[u // 4, :, (u % 4) * 1024:(u % 4 + 1) * 1024]
            if u < 14:
                return w_gate0[:, (u - 12) * 1024:(u - 11) * 1024]
            if u < 22:
                return w_in[3 + (u - 14) // 4, :, ((u - 14) % 4) * 1024:((u - 14) % 4 + 1) * 1024]
            return w_out[(u - 22) // 5, :, ((u - 22) % 5) * 1024:((u - 22) % 5 + 1) * 1024]

        @block.sync
        def _(sp):
            for dst, src in ((ident[:], ident_d), (gn[:], gains), (snk[:], sink),
                             (res[:, 0:2, :].rearrange("p a b -> p (a b)"), mem_norm_g.to_broadcast([P, D_MODEL]))):
                sp.dma_start(dst, src).then_inc(const.sem, 16)
            for t in range(2):
                sp.dma_start(xt[:, t, :], mem[t * P:(t + 1) * P, :]).then_inc(x_full[t].sem, 16)
            for u in range(2):
                sp.dma_start(raw[:, u, :], w_kv[:, u * 1024:(u + 1) * 1024]).then_inc(raw_full[u].sem, 16)
            for dst, src in ((gx[:], norm_g.to_broadcast([P, D_MODEL])), (bias[:, 0], alibi[:, 0]),
                             (bias[:, 1], alibi[:, 1]), (bias[:, 2], alibi[:, 2])):
                sp.dma_start(dst, src).then_inc(const.sem, 16)
            for u in range(2, 4):
                sp.wait_ge(w_lo.sem, 2 * (u - 1))
                sp.dma_start(raw[:, u % 2, :], w_kv[:, u * 1024:(u + 1) * 1024]).then_inc(raw_full[u % 2].sem, 16)
            for t in range(2):
                sp.wait_ge(tp_full.sem, 2 * t + 2)
                sp.dma_start(xt[:, t, :], x[t * P:(t + 1) * P, :]).then_inc(x_full[t].sem, 16)
            for u in range(2):
                sp.wait_ge(w_lo.sem, 2 * (u + 3))
                sp.dma_start(raw[:, u, :], w_unit(u)).then_inc(raw_full[u].sem, 16)
            for t in range(2, 4):
                sp.wait_ge(tp_full.sem, 6 + 2 * (t - 2) + 2)
                sp.dma_start(xt[:, t % 2, :], x[t * P:(t + 1) * P, :]).then_inc(x_full[t % 2].sem, 16)

            with sp.Fori(0, BLOCKS) as b:
                for u in range(UNITS):
                    sp.wait_ge(w_lo.sem, w_lo.at(b, 2 * u + 2))
                    sp.dma_start(raw[:, u % 2, :], w_unit((u + 2) % UNITS)).then_inc(raw_full[u % 2].sem, 16)
                    if u in (21, 22, 25, 27):
                        t = (21, 22, 25, 27).index(u)
                        last_half = TP_INDEX[(48 + 4 * ((t - 2) % 4), 1)] + 1 - (0 if t >= 2 else len(TP_ORDER))
                        sp.wait_ge(tp_full.sem, tp_full.at(b, last_half))
                        sp.dma_start(xt[:, t % 2, :], x[bass.ds(b * BLOCK + (BLOCK + t * P), P), :]).then_inc(
                            x_full[t % 2].sem, 16)
                    if u in (23, 30):
                        o = (23, 30).index(u)
                        sp.wait_ge(stored.sem, stored.at(b, 64 * o))
                        sp.dma_start(res[:], x[bass.ds(b * BLOCK, BLOCK), o * 512:(o + 1) * 512].rearrange(
                            "(t p) n -> p t n", p=P)).then_inc(res_full.sem, 16)
                    if u in (28, 31):
                        o = (28, 31).index(u)
                        for t in range(TILES):
                            sp.wait_ge(o_done.sem, o_done.at(b, 4 * o + t + 1))
                            sp.dma_start(out[bass.ds(b * BLOCK + t * P, P), o * 512:(o + 1) * 512],
                                         res[:, t, :]).then_inc(stored.sem, 16)
            sp.wait_ge(stored.sem, stored.at(BLOCKS, 0))
            for i in range(2):
                sp.wait_ge(raw_full[i].sem, raw_full[i].at(BLOCKS, 16))

        @block.gpsimd
        def _(pool):
            pool.memset(zeros[:], 0.0).then_inc(ready.sem, 1)
            pool.memset(half[:], -0.5).then_inc(ready.sem, 1)
            pool.memset(kTe[:, 0, 1, :], 0.0).then_inc(ready.sem, 1)
            pool.sem_inc(stored.sem, 64)
            pool.sem_inc(o_done.sem, 4)

            def power(out_, in_):
                return pool.tensor_tensor(out_, in_, half[:, 0:in_.shape[1]], ALU.pow)

            def x_power(k, val, before=None):
                pool.wait_ge(x_var.sem, val)
                if before is not None:
                    pool.wait_ge(x_n.sem, before)
                power(xr[:, k % 2:k % 2 + 1], xvar[:, k % 2:k % 2 + 1]).then_inc(x_r.sem, 1)

            for k in range(2):
                x_power(k, k + 1)
            for t in range(2):
                pool.wait_ge(u_var.sem, t + 1)
                power(ur[:, t, :], uvar[:, t, :]).then_inc(u_r.sem, 1)
            for k in range(2, 6):
                x_power(k, k + 1, k - 1)

            with pool.Fori(0, BLOCKS) as b:
                for n in range(STEPS):
                    for u in stage(n, 1):
                        pool.wait_ge(p_rinv.sem, p_rinv.at(b, u + 1))
                        segs = 2 if u < MEM_UNITS else 4
                        pv = ps[:, u % 3, :].rearrange("p (s k) -> p s k", s=segs)
                        pool.tensor_tensor(pv, pv, rinv[:, u % 3, 0:segs].unsqueeze(2).to_broadcast(
                            [P, segs, 512 // segs]), ALU.mult).then_inc(p_norm.sem, 1)
                    for s, e in enumerate(A_ENDS):
                        if n in (e + 1, e + 2):
                            for t in (2 * (n - e - 1), 2 * (n - e - 1) + 1):
                                pool.wait_ge(u_var.sem, u_var.at(b, 4 * s + t + 1))
                                power(ur[:, t, :], uvar[:, t, :]).then_inc(u_r.sem, 1)
                    if n in X_SQUARE:
                        k = X_SQUARE[n]
                        x_power(k, x_var.at(b, k + 1), x_n.at(b, k - 1))

        @block.scalar
        def _(act):
            def hi_of_chunk(slot, half_, wait):
                ring = wait[0]
                act.wait_ge(wait[1].sem, wait[2])
                if wait[3] is not None:
                    act.wait_ge(wait[3][0].sem, wait[3][1])
                act.activation(ws[:, ring, 0, :], raw[:, slot, half_ * 512:(half_ + 1) * 512],
                               ACT.Copy).then_inc(w_hi.sem, 1)

            def x_square(k, val, before):
                if before is not None:
                    act.wait_ge(x_sq.sem, before)
                act.wait_ge(x_full[k % 2].sem, val)
                act.activation(junk[:], xt[:, k % 2, :], ACT.Square,
                               accum_out=xss[:, k % 2:k % 2 + 1]).then_inc(x_sq.sem, 1)

            def x_hi(cols, h):
                return act.activation(xnT[:, 0, 4 * h:4 * h + 4, cols * P:(cols + 1) * P],
                                      tp[:].rearrange("p (k t) -> p k t", k=4), ACT.Copy)

            x_square(0, 16, None)
            x_square(1, 16, 1)
            for c in range(4):
                hi_of_chunk((c // 2) % 2, c % 2, (c % WRING, raw_full[(c // 2) % 2], 16, None))
            for t in range(2):
                for h in range(2):
                    act.wait_ge(tp_full.sem, 2 * t + h + 1)
                    x_hi(t, h).then_inc(tp_hi.sem, 1)
            for c in range(4, 8):
                hi_of_chunk((c // 2) % 2, c % 2, (c % WRING, raw_full[(c // 2) % 2], 32, (step_done, c - 3)))
            for t in range(2):
                act.wait_ge(acc_done.sem, t + 1)
                act.activation(u_tok[:, t, :], acc[t][:], ACT.Copy).then_inc(u_raw.sem, 1)
                act.wait_ge(u_raw.sem, t + 1)
                act.activation(mv[:, t, 0, :], u_tok[:, t, 256:512], ACT.Copy).then_inc(v_hi.sem, 1)
            for t in range(4):
                x_square(2 + t, 32 + 16 * (t // 2), 2 + t)
                for h in range(2):
                    act.wait_ge(tp_full.sem, 6 + 2 * t + h + 1)
                    x_hi(t, h).then_inc(tp_hi.sem, 1)
            for c in range(8, 8 + LEAD):
                hi_of_chunk((c // 2) % 2, c % 2, (c % WRING, raw_full[(c // 2) % 2], 48, (step_done, c - 3)))

            with act.Fori(0, BLOCKS) as b:
                for n in range(STEPS):
                    c = n + LEAD
                    slot = (c // 2) % 2
                    hi_of_chunk(slot, c % 2, (c % WRING, raw_full[slot], raw_full[slot].at(b, 16 * (c // 4 + 1)),
                                              step_over(b, c - WRING)))
                    if n in X_SQUARE:
                        k = X_SQUARE[n]
                        act.wait_ge(x_var.sem, x_var.at(b, k - 1))
                        x_square(k, x_full[k % 2].at(b, 16 * (k // 2 + 1)), x_sq.at(b, k))
                    for place in range(4):
                        key = (n, place)
                        if key in TP_HI:
                            kind, i, h = TP_AT[key]
                            act.wait_ge(tp_full.sem, tp_full.at(b, TP_INDEX[key] + 1))
                            if kind == "x":
                                x_hi(i, h).then_inc(tp_hi.sem, 1)
                            else:
                                act.activation(pT[:, i % 2, 0, :], tp[:], ACT.Copy).then_inc(tp_hi.sem, 1)
                    for u in stage(n, 0):
                        r = u % 3
                        segs = 2 if u < MEM_UNITS else 4
                        w = 512 // segs
                        act.wait_ge(sc_neg.sem, sc_neg.at(b, u + 1))
                        for s in range(segs):
                            last = act.activation(ps[:, r, s * w:(s + 1) * w], ps[:, r, s * w:(s + 1) * w], ACT.Exp,
                                                  bias=nmax[:, r, s:s + 1], scale=-1.0,
                                                  accum_out=den[:, r, s:s + 1])
                        if u >= MEM_UNITS:
                            act.wait_ge(sk_arg.sem, sk_arg.at(b, u - MEM_UNITS + 1))
                            last = act.activation(esk[:, r, :], dsk[:, r, :], ACT.Exp)
                        last.then_inc(p_exp.sem, 1)
                    if O_0 - 1 <= n < STEPS - 1:
                        i = n + 1 - O_0
                        over = step_over(b, n - 1)
                        act.wait_ge(y_prod.sem, y_prod.at(b, min(i, YT - 1) + 1))
                        act.wait_ge(over[0].sem, over[1])
                        act.activation(ys[:, i % 2, 0, :], y[:, i % YT, :], ACT.Copy).then_inc(y_hi.sem, 1)
                    if n in A_ENDS:
                        s = A_ENDS.index(n)
                        for t in range(TILES):
                            act.wait_ge(acc_done.sem, acc_done.at(b, 4 * s + t + 1))
                            act.activation(u_tok[:, t, :], acc[t][:], ACT.Copy).then_inc(u_raw.sem, 1)
                        if s == 0:
                            for t in range(TILES):
                                act.wait_ge(u_raw.sem, u_raw.at(b, t + 1))
                                act.activation(vO[:, t, 0, :], u_tok[:, t, P:2 * P], ACT.Copy).then_inc(v_hi.sem, 1)
                    if n in G_ENDS:
                        k0, kn = G_ENDS[n]
                        for t in range(kn):
                            act.wait_ge(acc_done.sem, acc_done.at(b, 12 + k0 + t + 1))
                            act.activation(gate[:, k0 + t, :], acc[t][:], ACT.Tanh, scale=0.5).then_inc(g_th.sem, 1)

        @block.vector
        def _(dve):
            dve.wait_ge(const.sem, N_CONST)
            dve.wait_ge(ready.sem, 3)
            dve.tensor_scalar(nsnk[:], snk[:], -1.0, None, ALU.mult).then_inc(ready.sem, 1)
            dve.tensor_scalar(gn[:, 0:2], gn[:, 0:2], HD ** -0.5, None, ALU.mult).then_inc(ready.sem, 1)
            dve.tensor_copy(vE[64:128, 0, :, :].rearrange("p a b -> p (a b)"), zeros[64:128, :]).then_inc(halo.sem, 1)
            dve.wait_ge(ready.sem, 5)

            def lo_of_chunk(slot, half_, ring, val):
                dve.wait_ge(w_hi.sem, val)
                dve.tensor_tensor(ws[:, ring, 1, :], raw[:, slot, half_ * 512:(half_ + 1) * 512],
                                  ws[:, ring, 0, :].bitcast(F32), ALU.subtract).then_inc(w_lo.sem, 1)

            def x_mean(k, val, before=None):
                dve.wait_ge(x_sq.sem, val)
                if before is not None:
                    dve.wait_ge(x_r.sem, before)
                dve.tensor_scalar(xvar[:, k % 2:k % 2 + 1], xss[:, k % 2:k % 2 + 1], 1.0 / D_MODEL, EPS,
                                  ALU.mult, ALU.add).then_inc(x_var.sem, 1)

            def x_scale(k, val, g):
                dve.wait_ge(x_r.sem, val)
                dve.scalar_tensor_tensor(out=xt[:, k % 2, :], in0=xt[:, k % 2, :], scalar=xr[:, k % 2:k % 2 + 1],
                                         in1=g, op0=ALU.mult, op1=ALU.mult).then_inc(x_n.sem, 1)

            def x_lo(cols, h, val):
                dve.wait_ge(tp_hi.sem, val)
                dve.tensor_tensor(xnT[:, 1, 4 * h:4 * h + 4, cols * P:(cols + 1) * P],
                                  tp[:].rearrange("p (k t) -> p k t", k=4),
                                  xnT[:, 0, 4 * h:4 * h + 4, cols * P:(cols + 1) * P].bitcast(F32),
                                  ALU.subtract).then_inc(tp_free.sem, 1)

            def head_squares(t, raw_val, base_val):
                dve.wait_ge(u_raw.sem, raw_val)
                if t or base_val.__class__ is not int:
                    dve.wait_ge(u_ss.sem, base_val)
                dve.tensor_tensor(usq[:], u_tok[:, t, :], u_tok[:, t, :], ALU.mult).then_inc(u_sq.sem, 1)
                dve.wait_ge(u_sq.sem, base_val + 1)
                dve.tensor_reduce(uss[:, t, :], usq[:].rearrange("p (h d) -> p h d", d=HD), AX.X,
                                  ALU.add).then_inc(u_ss.sem, 1)
                dve.wait_ge(u_ss.sem, base_val + 1)
                dve.tensor_scalar(uvar[:, t, :], uss[:, t, :], 1.0 / HD, EPS, ALU.mult, ALU.add).then_inc(u_var.sem, 1)

            def scale_heads(t, h0, h1):
                v = u_tok[:, t, h0 * HD:h1 * HD].rearrange("p (h d) -> p h d", d=HD)
                return dve.tensor_tensor(v, v, ur[:, t, h0:h1].unsqueeze(2).to_broadcast([P, h1 - h0, HD]), ALU.mult)

            for k in range(2):
                x_mean(k, k + 1)
            for k in range(2):
                x_scale(k, k + 1, res[:, 0:2, :].rearrange("p a b -> p (a b)"))
            for c in range(4):
                lo_of_chunk((c // 2) % 2, c % 2, c % WRING, c + 1)
            for e in range(4):
                x_lo(e // 2, e % 2, e + 1)
            for c in range(4, 8):
                lo_of_chunk((c // 2) % 2, c % 2, c % WRING, c + 1)
            for t in range(2):
                head_squares(t, t + 1, t)
            for t in range(2):
                dve.wait_ge(u_r.sem, t + 1)
                scale_heads(t, 0, 4).then_inc(u_n.sem, 1)
                dve.wait_ge(v_hi.sem, t + 1)
                dve.tensor_tensor(mv[:, t, 1, :], u_tok[:, t, 256:512], mv[:, t, 0, :].bitcast(F32),
                                  ALU.subtract).then_inc(v_lo.sem, 1)
            for t in range(2):
                dve.wait_ge(tp_full.sem, 4 + t + 1)
                dve.tensor_scalar(mkT[:, :, t * P:(t + 1) * P], tp[:, 0:256].rearrange("p (k t) -> p k t", k=2),
                                  gn[:, 3:4], None, ALU.mult).then_inc(tp_free.sem, 1)
            for t in range(4):
                x_mean(2 + t, 2 + t + 1, t + 1)
                x_scale(2 + t, 2 + t + 1, gx[:])
                for h in range(2):
                    x_lo(t, h, 4 + 2 * t + h + 1)
            for c in range(8, 8 + LEAD):
                lo_of_chunk((c // 2) % 2, c % 2, c % WRING, c + 1)

            def scores(b, u):
                r = u % 3
                if u < MEM_UNITS:
                    for s in range(2):
                        last = dve.tensor_tensor_reduce(
                            ps[:, r, s * 256:(s + 1) * 256], sc[u % 2][:, s * 256:(s + 1) * 256], zeros[:], -1.0, BIG,
                            ALU.add, ALU.min, nmax[:, r, s:s + 1])
                    last.then_inc(sc_neg.sem, 1)
                    return
                c, g = (u - MEM_UNITS) // 2, (u - MEM_UNITS) % 2
                table = 2 if c == 0 else c % 2
                for s in range(4):
                    pair = 4 * g + s
                    last = dve.tensor_tensor_reduce(
                        ps[:, r, s * P:(s + 1) * P], sc[u % 2][:, s * P:(s + 1) * P], bias[:, table, pair, :], -1.0,
                        nsnk[:, pair:pair + 1], ALU.add, ALU.min, nmax[:, r, s:s + 1])
                last.then_inc(sc_neg.sem, 1)
                dve.wait_ge(sc_neg.sem, sc_neg.at(b, u + 1))
                dve.tensor_tensor(dsk[:, r, :], nmax[:, r, :], nsnk[:, 4 * g:4 * g + 4],
                                  ALU.subtract).then_inc(sk_arg.sem, 1)

            def denominators(b, u):
                r = u % 3
                segs = 2 if u < MEM_UNITS else 4
                dve.wait_ge(p_exp.sem, p_exp.at(b, u + 1))
                if u >= MEM_UNITS:
                    dve.tensor_tensor(dtot[:, r, :], den[:, r, :], esk[:, r, :], ALU.add).then_inc(d_sum.sem, 1)
                    dve.wait_ge(d_sum.sem, d_sum.at(b, u - MEM_UNITS + 1))
                total = den if u < MEM_UNITS else dtot
                dve.reciprocal(rinv[:, r, 0:segs], total[:, r, 0:segs]).then_inc(p_rinv.sem, 1)

            with dve.Fori(0, BLOCKS) as b:
                for n in range(STEPS):
                    for u in stage(n, 1):
                        denominators(b, u)
                    for u in stage(n, 0):
                        dve.wait_ge(sc_full.sem, sc_full.at(b, u + 1))
                    c = n + LEAD
                    lo_of_chunk((c // 2) % 2, c % 2, c % WRING, w_hi.at(b, c + 1))
                    for u in stage(n, 0):
                        scores(b, u)
                    for s, e in enumerate(A_ENDS):
                        if n in (e + 2, e + 3):
                            for t in (2 * (n - e - 2), 2 * (n - e - 2) + 1):
                                dve.wait_ge(u_r.sem, u_r.at(b, 4 * s + t + 1))
                                if s == 0:
                                    scale_heads(t, 0, 2)
                                    scale_heads(t, 4, 8).then_inc(u_n.sem, 1)
                                else:
                                    scale_heads(t, 0, 8).then_inc(u_n.sem, 1)
                        if n in (e + 1, e + 2):
                            for t in (2 * (n - e - 1), 2 * (n - e - 1) + 1):
                                head_squares(t, u_raw.at(b, 4 * s + t + 1), u_ss.at(b, 4 * s + t))
                                if s == 0:
                                    dve.wait_ge(v_hi.sem, v_hi.at(b, t + 1))
                                    dve.tensor_tensor(vO[:, t, 1, :], u_tok[:, t, P:2 * P],
                                                      vO[:, t, 0, :].bitcast(F32), ALU.subtract).then_inc(v_lo.sem, 1)
                                    dve.wait_ge(v_lo.sem, v_lo.at(b, t + 1))
                                    if t == TILES - 1:
                                        dve.wait_ge(halo.sem, halo.at(b, 0))
                                    dve.tensor_copy(vE[0:64, t], vO[0:64, t].bitcast(F32))
                                    dve.tensor_copy(vE[64:128, t + 1],
                                                    vO[64:128, t].bitcast(F32)).then_inc(v_even.sem, 1)
                    if n in X_SQUARE:
                        k = X_SQUARE[n]
                        x_mean(k, x_sq.at(b, k + 1), x_r.at(b, k - 1))
                    if n in X_SCALE:
                        k = X_SCALE[n]
                        x_scale(k, x_r.at(b, k + 1), gx[:])
                    for place in range(4):
                        key = (n, place)
                        if key not in TP_INDEX:
                            continue
                        kind, i, h = TP_AT[key]
                        if kind == "x":
                            x_lo(i, h, tp_hi.at(b, TP_HI[key] + 1))
                        elif kind == "p":
                            dve.wait_ge(tp_hi.sem, tp_hi.at(b, TP_HI[key] + 1))
                            dve.tensor_tensor(pT[:, i % 2, 1, :], tp[:], pT[:, i % 2, 0, :].bitcast(F32),
                                              ALU.subtract).then_inc(tp_free.sem, 1)
                        else:
                            s, t = i, h
                            dve.wait_ge(tp_full.sem, tp_full.at(b, TP_INDEX[key] + 1))
                            if s == 0:
                                dve.tensor_scalar(kTo[:, t, :], tp[:, 0:P], gn[:, 2:3], None, ALU.mult)
                                if t == 0:
                                    dve.wait_ge(halo.sem, halo.at(b, 0))
                                dve.tensor_scalar(kTe[:, t, 0, :], tp[:, 0:CHUNK], gn[:, 2:3], None, ALU.mult)
                                dve.tensor_scalar(kTe[:, t + 1, 1, :], tp[:, CHUNK:P], gn[:, 2:3], None, ALU.mult)
                                dve.tensor_scalar(mqT[:, :, t * P:(t + 1) * P],
                                                  tp[:, P:3 * P].rearrange("p (k t) -> p k t", k=2),
                                                  gn[:, 1:2], None, ALU.mult).then_inc(tp_free.sem, 1)
                            else:
                                j0 = 4 * (s - 1)
                                for cc in range(2):
                                    last = dve.tensor_scalar(
                                        qT[:, 2 * t + cc, j0:j0 + 4, :],
                                        tp[:].rearrange("p (j c q) -> p j c q", c=2, q=CHUNK)[:, :, cc, :],
                                        gn[:, 0:1], None, ALU.mult)
                                last.then_inc(tp_free.sem, 1)
                    for u in stage(n, 3):
                        dve.wait_ge(y_full.sem, y_full.at(b, u + 1))
                        if u < MEM_UNITS:
                            t, a = u // 2, u % 2
                            dve.tensor_copy(y[0:64, a, t * P:(t + 1) * P], yb[0:64, 0:P])
                            dve.tensor_copy(y[64:128, a, t * P:(t + 1) * P], yb[64:128, P:2 * P]).then_inc(y_free.sem, 1)
                        else:
                            c, g = (u - MEM_UNITS) // 2, (u - MEM_UNITS) % 2
                            dve.tensor_copy(y[64 * g:64 * g + 64, 2:10, c * CHUNK:(c + 1) * CHUNK],
                                            yb[64 * g:64 * g + 64, :].rearrange("p (j q) -> p j q", q=CHUNK)).then_inc(
                                                y_free.sem, 1)
                    if n in Y_GATE:
                        k = Y_GATE[n]
                        dve.wait_ge(y_free.sem, y_free.at(b, MEM_UNITS if k < 2 else N_UNITS))
                        dve.wait_ge(g_done.sem, g_done.at(b, 2 if k < 2 else YT))
                        dve.scalar_tensor_tensor(out=y[:, k, :], in0=gate[:, k, :], scalar=0.5, in1=y[:, k, :],
                                                 op0=ALU.mult, op1=ALU.mult).then_inc(y_prod.sem, 1)
                    if O_0 - 1 <= n < STEPS - 1:
                        i = n + 1 - O_0
                        dve.wait_ge(y_hi.sem, y_hi.at(b, i + 1))
                        dve.tensor_tensor(ys[:, i % 2, 1, :], y[:, i % YT, :], ys[:, i % 2, 0, :].bitcast(F32),
                                          ALU.subtract).then_inc(y_lo.sem, 1)
                    if n in G_ENDS:
                        k0, kn = G_ENDS[n]
                        for t in range(kn):
                            dve.wait_ge(g_th.sem, g_th.at(b, k0 + t + 1))
                            dve.scalar_tensor_tensor(out=gate[:, k0 + t, :], in0=gate[:, k0 + t, :], scalar=1.0,
                                                     in1=acc[t][:], op0=ALU.add, op1=ALU.mult).then_inc(g_done.sem, 1)
                    if n in O_ENDS:
                        o = O_ENDS[n]
                        dve.wait_ge(res_full.sem, res_full.at(b, 16 * (o + 1)))
                        for t in range(TILES):
                            dve.wait_ge(acc_done.sem, acc_done.at(b, 22 + 4 * o + t + 1))
                            dve.tensor_tensor(res[:, t, :], acc[t][:], res[:, t, :], ALU.add).then_inc(o_done.sem, 1)
                    if n == 48:
                        dve.wait_ge(y_full.sem, y_full.at(b, N_UNITS))
                        dve.wait_ge(tp_free.sem, tp_free.at(b, TP_INDEX[(11, 2)] + 1))
                        dve.tensor_copy(bias[:, 2], bias[:, 0])
                        dve.tensor_copy(vE[64:128, 0], vE[64:128, TILES].bitcast(F32))
                        dve.tensor_copy(kTe[:, 0, 1, :], kTe[:, TILES, 1, :]).then_inc(halo.sem, 1)

        @block.tensor
        def _(pe):
            PASSES = ((0, 0), (0, 1), (1, 0))

            def x_transposes(k, h, val, free):
                pe.wait_ge(x_n.sem, val)
                if free is not None:
                    pe.wait_ge(tp_free.sem, free)
                for j in range(4):
                    last = pe.transpose(tp[:, j * P:(j + 1) * P], xt[:, k % 2, (4 * h + j) * P:(4 * h + j + 1) * P],
                                        ident[:])
                last.then_inc(tp_full.sem, 1)

            pe.wait_ge(const.sem, N_CONST)
            for t in range(2):
                for h in range(2):
                    e = 2 * t + h
                    x_transposes(t, h, t + 1, e if e else None)
            pe.wait_ge(tp_free.sem, 4)
            for k in range(KT):
                pe.wait_ge(w_lo.sem, k + 1)
                for t in range(2):
                    for i, (a, w) in enumerate(PASSES):
                        last = pe.matmul(acc[t][:], xnT[:, a, k, t * P:(t + 1) * P], ws[:, k % WRING, w, :],
                                         start=(k == 0 and i == 0), stop=(k == KT - 1 and i == 2))
                    if k == KT - 1:
                        last.then_inc(acc_done.sem, 1)
                if k < KT - 1:
                    last.then_inc(step_done.sem, 1)
            for t in range(2):
                pe.wait_ge(u_n.sem, t + 1)
                pe.wait_ge(tp_free.sem, 4 + t)
                for j in range(2):
                    last = pe.transpose(tp[:, j * P:(j + 1) * P], u_tok[:, t, j * P:(j + 1) * P], ident[:])
                last.then_inc(tp_full.sem, 1)
            for t in range(4):
                for h in range(2):
                    x_transposes(2 + t, h, 2 + t + 1, 6 + 2 * t + h)

            def qk(b, u):
                s = sc[u % 2]
                if u >= 2:
                    pe.wait_ge(sc_neg.sem, sc_neg.at(b, u - 1))
                if u == MEM_UNITS:
                    pe.wait_ge(halo.sem, halo.at(b, 0))
                if u < MEM_UNITS:
                    t, a = u // 2, u % 2
                    pe.wait_ge(tp_free.sem, tp_free.at(b, TP_INDEX[(10 + t // 2, 2 * (t % 2))] + 1))
                    h = slice(64 * a, 64 * a + 64)
                    for hp in range(2):
                        last = pe.matmul(s[:, hp * 256:(hp + 1) * 256], mqT[h, hp, t * P:(t + 1) * P], mkT[h, hp, :],
                                         start=True, stop=True)
                else:
                    c, g = (u - MEM_UNITS) // 2, (u - MEM_UNITS) % 2
                    t = c // 2
                    pe.wait_ge(tp_free.sem, tp_free.at(b, TP_INDEX[(26 + t // 2, 2 * (t % 2))] + 1))
                    h = slice(64 * g, 64 * g + 64)
                    keys = kTo[h, t, :] if c % 2 else kTe[h, t, :, :].rearrange("p a b -> p (a b)")
                    for p in range(4):
                        last = pe.matmul(s[:, p * P:(p + 1) * P],
                                         qT[h, c, 2 * p:2 * p + 2, :].rearrange("p a b -> p (a b)"), keys,
                                         start=True, stop=True)
                last.then_inc(sc_full.sem, 1)

            def p_transposes(b, u):
                pe.wait_ge(p_norm.sem, p_norm.at(b, u + 1))
                for j in range(4):
                    i = (j % 2) * 2 + j // 2 if u < MEM_UNITS else j
                    last = pe.transpose(tp[:, j * P:(j + 1) * P], ps[:, u % 3, i * P:(i + 1) * P], ident[:])
                return last

            def pv(b, u):
                r = u % 2
                key = next(k for k in TP_ORDER if TP_AT[k] == ("p", u, 0))
                pe.wait_ge(tp_free.sem, tp_free.at(b, TP_INDEX[key] + 1))
                if u > 0:
                    pe.wait_ge(y_free.sem, y_free.at(b, u))
                if u < MEM_UNITS:
                    a = u % 2
                    for kt in range(2):
                        for i, (v, p) in enumerate(PASSES):
                            last = pe.matmul(yb[:, 0:256], mv[:, kt, v, a * P:(a + 1) * P],
                                             pT[:, r, p, kt * 256:(kt + 1) * 256],
                                             start=(kt == 0 and i == 0), stop=(kt == 1 and i == 2))
                else:
                    c = (u - MEM_UNITS) // 2
                    v_ = vO if c % 2 else vE
                    pe.wait_ge(v_even.sem, v_even.at(b, c // 2 + 1))
                    for i, (v, p) in enumerate(PASSES):
                        last = pe.matmul(yb[:], v_[:, c // 2, v, :], pT[:, r, p, :], start=(i == 0), stop=(i == 2))
                last.then_inc(y_full.sem, 1)

            def tp_event(b, n, place):
                key = (n, place)
                if key not in TP_INDEX:
                    return
                kind, i, h = TP_AT[key]
                free = tp_free.at(b, TP_INDEX[key])
                if kind == "x":
                    x_transposes(i, h, x_n.at(b, i + 1), free)
                    return
                pe.wait_ge(tp_free.sem, free)
                if kind == "p":
                    p_transposes(b, i).then_inc(tp_full.sem, 1)
                    return
                s, t = i, h
                pe.wait_ge(u_n.sem, u_n.at(b, 4 * s + t + 1))
                cols = (0, 2, 3) if s == 0 else (0, 1, 2, 3)
                for j, cblk in enumerate(cols):
                    last = pe.transpose(tp[:, j * P:(j + 1) * P], u_tok[:, t, cblk * P:(cblk + 1) * P], ident[:])
                last.then_inc(tp_full.sem, 1)

            def group(b, n, t):
                ring = n % WRING
                if n < G_0:
                    k, K = n % 8, KT
                    return [(xnT[:, a, k, t * P:(t + 1) * P], ws[:, ring, w, :]) for a, w in PASSES], k == 0, k == K - 1
                if n < G_1:
                    m = n - G_0
                    return [(ws[:, ring, w, kk * 256 + t * P:kk * 256 + (t + 1) * P], xnT[:, a, 2 * m + kk, :])
                            for kk in range(2) for w, a in PASSES], m == 0, m == 3
                if n < O_0:
                    k = (n - G_1) % 8
                    return [(ws[:, ring, w, t * P:(t + 1) * P], xnT[:, a, k, :]) for w, a in PASSES], k == 0, k == 7
                k = (n - O_0) % YT
                yr = (n - O_0) % 2
                return [(ys[:, yr, a, t * P:(t + 1) * P], ws[:, ring, w, :]) for a, w in PASSES], k == 0, k == YT - 1

            with pe.Fori(0, BLOCKS) as b:
                for n in range(STEPS):
                    pe.wait_ge(w_lo.sem, w_lo.at(b, n + 1))
                    if n >= O_0:
                        pe.wait_ge(y_lo.sem, y_lo.at(b, n - O_0 + 1))
                    if n == 0:
                        pe.wait_ge(tp_free.sem, tp_free.at(b, 0))
                    tiles = 2 if G_0 <= n < G_1 else 4
                    for t in range(4):
                        if t == 0:
                            for u in stage(n, 0):
                                qk(b, u)
                        tp_event(b, n, t)
                        if t == 3:
                            for u in stage(n, 3):
                                pv(b, u)
                        if t >= tiles:
                            continue
                        ops, first, final = group(b, n, t)
                        if first:
                            who, how_many = bank_free(n, t)
                            cnt = {"o_done": o_done, "u_raw": u_raw, "g_done": g_done}[who]
                            pe.wait_ge(cnt.sem, cnt.at(b, how_many))
                        for i, (lhs, rhs) in enumerate(ops):
                            last = pe.matmul(acc[t][:], lhs, rhs, start=(first and i == 0),
                                             stop=(final and i == len(ops) - 1))
                        if final:
                            last.then_inc(acc_done.sem, 1)
                    if not final:
                        last.then_inc(step_done.sem, 1)


def head_columns():
    import numpy as np

    d = np.arange(HD)
    mem_cols = [N_HEADS * HD + h * HD + d for h in (0, 2, 1, 3)]
    win_cols = [h * HD + d for j in range(PAIRS) for h in (j, PAIRS + j)]
    return np.concatenate(mem_cols), np.concatenate(win_cols)


def alibi_table():
    import numpy as np

    slopes = np.float32(2.0) ** (np.float32(-8.0) * np.arange(1, N_HEADS + 1, dtype=np.float32) / np.float32(N_HEADS))
    q = np.arange(CHUNK)[:, None]
    k = np.arange(2 * CHUNK)[None, :]
    dist = np.abs(q - k + CHUNK).astype(np.float32)
    t = np.zeros((P, 3, PAIRS, P), np.float32)
    for pair in range(PAIRS):
        for a in range(2):
            rows = slice(a * CHUNK, (a + 1) * CHUNK)
            odd = -slopes[2 * pair + a] * dist
            even = np.concatenate([odd[:, CHUNK:], odd[:, :CHUNK]], axis=1)
            t[rows, 0, pair] = even
            t[rows, 1, pair] = odd
            t[rows, 2, pair] = even
            t[rows, 2, pair, CHUNK:] = -1e30
    return t


def kernel(**inputs):
    import numpy as np
    import concourse.bacc as bacc
    from concourse.bass_utils import run_bass_kernel_spmd

    f32 = np.float32
    x = np.ascontiguousarray(inputs["x"]).reshape(SEQ, D_MODEL)
    mem = np.ascontiguousarray(inputs["mem"]).reshape(N_MEM, D_MODEL)
    w_in = np.asarray(inputs["a_w_in"])[0]
    w_out = np.asarray(inputs["w_out"])[0]
    mem_cols, win_cols = head_columns()
    kv0 = N_HEADS * HD
    mq0 = kv0 + 2 * KV_HEADS * HD
    g0 = mq0 + MEM_HEADS * HD
    w_kv = np.asarray(inputs["mem_w_kv"])
    gate_cols = g0 + np.concatenate([mem_cols, win_cols])

    def chunks(w):
        k, n = w.shape
        return w.reshape(k // P, P, n).transpose(1, 0, 2).reshape(P, -1)

    slices = [w_in[:, kv0:g0], w_in[:, win_cols[:512]], w_in[:, win_cols[512:]],
              w_in[:, gate_cols[256:768]], w_in[:, gate_cols[768:]]]
    w_rows = w_out[np.concatenate([mem_cols, win_cols])]
    gains = [inputs["a_q_norm_g"][0], inputs["mem_q_norm_g"][0], inputs["a_k_norm_g"][0], inputs["mem_k_norm_g"]]
    arrays = {
        "x": np.concatenate([x, np.zeros((BLOCK, D_MODEL), f32)]),
        "mem": mem,
        "w_in": np.stack([chunks(w) for w in slices]),
        "w_gate0": chunks(w_in[:, gate_cols[:256]]),
        "w_out": np.stack([chunks(w_rows[:, :512]), chunks(w_rows[:, 512:])]),
        "w_kv": chunks(np.concatenate([w_kv[:, :256], w_kv[:, mem_cols - kv0 + 256]], axis=1)),
        "norm_g": np.asarray(inputs["norm_g"]).reshape(1, D_MODEL),
        "mem_norm_g": np.asarray(inputs["mem_norm_g"]).reshape(1, D_MODEL),
        "gains": np.stack([np.tile(np.asarray(g), 2) for g in gains], axis=1),
        "sink": np.repeat(np.asarray(inputs["a_sink"])[0].reshape(PAIRS, 2).T, CHUNK, axis=0),
        "ident": np.eye(P, dtype=f32),
        "alibi": alibi_table(),
    }
    nc = bacc.Bacc("TRN2", target_bir_lowering=False, num_devices=1)
    feeds, args = {}, []
    for name, a in arrays.items():
        a = np.ascontiguousarray(a)
        feeds[f"in_{name}"] = a
        args.append(nc.dram_tensor(f"in_{name}", a.shape, F32, kind="ExternalInput").ap())
    args.append(nc.dram_tensor("out_0", (SEQ, D_MODEL), F32, kind="ExternalOutput").ap())
    encoder_layer(nc, *args)
    r = run_bass_kernel_spmd(nc, [feeds], core_ids=[0])
    return r.results[0]["out_0"].reshape(1, SEQ, D_MODEL)
```

```python
from contextlib import ExitStack

import concourse.bass as bass
from concourse import mybir

F32 = mybir.dt.float32
F32R = mybir.dt.float32r
BF16 = mybir.dt.bfloat16
ALU = mybir.AluOpType
ACT = mybir.ActivationFunctionType
AX = mybir.AxisListType

P = 128
D_MODEL, SEQ, N_MEM = 1024, 2048, 256
HD = 64
CHUNK = 64
N_HEADS, KV_HEADS, MEM_HEADS = 16, 2, 4
EPS = 1e-6
BLOCK = 512
BLOCKS = SEQ // BLOCK
TILES = BLOCK // P
KT = D_MODEL // P
YT = (N_HEADS + MEM_HEADS) // 2
PAIRS = N_HEADS // 2
CPB = BLOCK // CHUNK
BIG = 3.0e38

A_KV, A_Q0, A_Q1 = 0, 8, 16
G_0, G_1, G_2 = 24, 28, 36
O_0, O_1 = 44, 54
STEPS = 64
LEAD = 3
WRING = 4
YRING = 3
UNITS = STEPS // 2
A_ENDS = (7, 15, 23)
G_ENDS = {27: (0, 2), 35: (2, 4), 43: (6, 4)}
O_ENDS = {53: 0, 63: 1}
FINALS = (*A_ENDS, *G_ENDS, *O_ENDS)
PRO_CHUNKS = KT

MEM_UNITS = 8
WIN_UNITS = 16
N_UNITS = MEM_UNITS + WIN_UNITS
T_LAG, PV_LAG = 2, 3
SLOTS = {}
for i in range(MEM_UNITS + PV_LAG):
    SLOTS[2 * 12 + 2 * i] = (0, MEM_UNITS, i)
for i in range(WIN_UNITS + PV_LAG):
    SLOTS[2 * 28 + round(i * 31 / (WIN_UNITS + PV_LAG - 1))] = (MEM_UNITS, WIN_UNITS, i)


def stage(half_step, lag):
    if half_step not in SLOTS:
        return []
    first, units, i = SLOTS[half_step]
    return [first + i - lag] if 0 <= i - lag < units else []


TP_AT = {(2, 1): ("r", 0, 0)}
for s, e in enumerate(A_ENDS):
    for t in range(TILES):
        TP_AT[(e + 4 + t // 2, 2 * (t % 2))] = ("q", s, t)
for hs in SLOTS:
    for u in stage(hs, T_LAG):
        TP_AT[(hs // 2, 2 * (hs % 2) + 1)] = ("p", u, 0)
TP_ORDER = sorted(TP_AT)
TP_INDEX = {key: i for i, key in enumerate(TP_ORDER)}
TP_OF = {TP_AT[key]: TP_INDEX[key] for key in TP_ORDER}
TP_HI = {}
for key in TP_ORDER:
    if TP_AT[key][0] == "p":
        TP_HI[key] = len(TP_HI)
PRO_TP = 2
X_SPLIT = {46 + 2 * k: k for k in range(KT)}
X_SQUARE = {47: 0, 51: 1, 55: 2, 59: 3}
Y_GATE = {41: 0, 42: 1, **{42 + k: k for k in range(2, YT)}}


def banks(n):
    return sum(2 if e == 27 else 4 for e in FINALS if e <= n)


def bank_free(n, t):
    return {A_KV: ("o_done", t - 3), A_Q0: ("u_raw", t + 1), A_Q1: ("u_raw", 4 + t + 1), G_0: ("u_raw", 8 + t + 1),
            G_1: ("g_raw", t + 1) if t < 2 else ("u_raw", 8 + t + 1), G_2: ("g_raw", 2 + t + 1),
            O_0: ("g_raw", 6 + t + 1), O_1: ("o_done", t + 1)}[n]


class Count:
    def __init__(self, sem, per, base):
        self.sem, self.per, self.base = sem, per, base

    def at(self, turn, n):
        return turn * self.per + (self.base + n)


def encoder_layer(nc, x, xT, mem, memT, w_in, w_gate0, w_out, w_kv, norm_gains, gains, sink, ident_d, alibi, out):
    ctx = ExitStack()
    with ctx:
        def sb(name, shape, dt=F32):
            return ctx.enter_context(nc.sbuf_tensor(name, shape, dt))

        def count(name, per, base):
            return Count(ctx.enter_context(nc.semaphore(name)), per, base)

        raw = sb("raw", [P, 2, 1024])
        ws = sb("w_split", [P, WRING, 2, 512], F32R)
        xnT = sb("xnT", [P, 2, KT, BLOCK], F32R)
        xraw = sb("xraw", [P, 2, 512])
        xt = sb("xt", [P, D_MODEL])
        gx = sb("gx", [P, 2, KT])
        u_tok = sb("u_tok", [P, TILES, 512])
        tmp = sb("tmp", [P, 2, 512])
        qT = sb("qT", [P, CPB, 8, CHUNK])
        mqT = sb("mqT", [P, 2, BLOCK])
        kTo = sb("kT_odd", [P, TILES, P])
        kTe = sb("kT_even", [P, TILES + 1, 2, CHUNK])
        vO = sb("v_odd", [P, TILES, 2, P], F32R)
        vE = sb("v_even", [P, TILES + 1, 2, P], F32R)
        mkT = sb("mkT", [P, 2, N_MEM])
        mv = sb("mv", [P, 2, 2, 256], F32R)
        ps = sb("p_score", [P, 3, 512])
        pT = sb("pT", [P, 2, 2, 512], F32R)
        y = sb("y", [P, YT, BLOCK])
        gate = sb("gate", [P, YT, BLOCK])
        ys = sb("y_split", [P, YRING, 2, BLOCK], F32R)
        res = sb("res", [P, TILES, 512])
        bias = sb("alibi_sb", [P, 3, PAIRS, P])
        ident = sb("ident", [P, P])
        zeros = sb("zeros", [P, 256])
        gn = sb("gn", [P, 4])
        snk = sb("snk", [P, PAIRS])
        nsnk = sb("nsnk", [P, PAIRS])
        half = sb("half", [P, 8])
        ones = sb("ones", [P, P])
        rbc = sb("rbc", [P, BLOCK])
        xss = sb("xss", [P, 6])
        xvar = sb("xvar", [P, 6])
        xr = sb("xr", [P, 6])
        uss = sb("uss", [P, TILES, 8])
        uvar = sb("uvar", [P, TILES, 8])
        ur = sb("ur", [P, TILES, 8])
        nmax = sb("nmax", [P, 3, 4])
        dsk = sb("dsk", [P, 3, 4])
        esk = sb("esk", [P, 3, 4])
        den = sb("den", [P, 3, 4])
        dtot = sb("dtot", [P, 3, 4])
        rinv = sb("rinv", [P, 3, 4])

        acc = [ctx.enter_context(nc.psum_tensor(f"acc{i}", [P, 512], F32)) for i in range(TILES)]
        tp = ctx.enter_context(nc.psum_tensor("tp", [P, 512], F32))
        sc = [ctx.enter_context(nc.psum_tensor(f"sc{i}", [P, 512], F32)) for i in range(2)]
        yb = ctx.enter_context(nc.psum_tensor("yb", [P, 512], F32))

        raw_full = [count(f"raw_full{i}", 16 * UNITS // 2, 32) for i in range(2)]
        w_hi = count("w_hi", STEPS, PRO_CHUNKS)
        w_lo = count("w_lo", STEPS, PRO_CHUNKS)
        step_done = count("step_done", STEPS - len(FINALS), PRO_CHUNKS - 1)
        acc_done = count("acc_done", 30, 2)
        xt_full = count("xt_full", 64, 96)
        xraw_full = [count(f"xraw_full{i}", 64, 96) for i in range(2)]
        x_hi = count("x_hi", KT, 2 * KT)
        x_lo = count("x_lo", KT, 2 * KT)
        x_sq = count("x_sq", 4, 6)
        x_var = count("x_var", 4, 6)
        x_r = count("x_r", 4, 6)
        r_diag = count("r_diag", 1, 0)
        u_raw = count("u_raw", 12, 2)
        u_sq = count("u_sq", 12, 2)
        u_ss = count("u_ss", 12, 2)
        u_var = count("u_var", 12, 2)
        u_r = count("u_r", 12, 2)
        u_n = count("u_n", 12, 2)
        v_hi = count("v_hi", 4, 2)
        v_lo = count("v_lo", 4, 2)
        v_even = count("v_even", 1, 0)
        halo = count("halo", 1, 1)
        tp_full = count("tp_full", len(TP_ORDER), PRO_TP)
        tp_hi = count("tp_hi", len(TP_HI), 0)
        tp_free = count("tp_free", len(TP_ORDER), PRO_TP)
        sc_full = count("sc_full", N_UNITS, 0)
        sc_neg = count("sc_neg", N_UNITS, 0)
        sk_arg = count("sk_arg", WIN_UNITS, 0)
        p_exp = count("p_exp", N_UNITS, 0)
        d_sum = count("d_sum", WIN_UNITS, 0)
        p_rinv = count("p_rinv", N_UNITS, 0)
        p_norm = count("p_norm", N_UNITS, 0)
        y_full = count("y_full", N_UNITS, 0)
        y_free = count("y_free", N_UNITS, 0)
        g_raw = count("g_raw", YT, 0)
        g_th = count("g_th", YT, 0)
        g_done = count("g_done", YT, 0)
        y_prod = count("y_prod", YT, 0)
        y_hi = count("y_hi", 2 * YT, 0)
        y_lo = count("y_lo", 2 * YT, 0)
        res_full = count("res_full", 32, 0)
        o_done = count("o_done", 8, 4)
        stored = count("stored", 128, 64)
        const = count("const", 0, 0)
        ready = count("ready", 0, 0)
        N_CONST = 16 * 7

        def step_over(b, n):
            if n in FINALS or n == -1:
                return acc_done, acc_done.at(b, banks(n))
            return step_done, step_done.at(b, sum(m not in FINALS for m in range(n + 1)))

        block = ctx.enter_context(nc.Block())

        def w_unit(u):
            if u < 12:
                return w_in[u // 4, :, (u % 4) * 1024:(u % 4 + 1) * 1024]
            if u < 14:
                return w_gate0[:, (u - 12) * 1024:(u - 11) * 1024]
            if u < 22:
                return w_in[3 + (u - 14) // 4, :, ((u - 14) % 4) * 1024:((u - 14) % 4 + 1) * 1024]
            return w_out[(u - 22) // 5, :, ((u - 22) % 5) * 1024:((u - 22) % 5 + 1) * 1024]

        @block.sync
        def _(sp):
            def load(dst, src, signal):
                sp.dma_start(dst, src).then_inc(signal.sem, 16)

            for i in range(2):
                load(xraw[:, i, :], memT[:, i * 512:(i + 1) * 512], xraw_full[i])
                load(raw[:, i, :], w_kv[:, i * 1024:(i + 1) * 1024], raw_full[i])
                if i == 0:
                    load(gx[:].rearrange("p a b -> p (a b)"), norm_gains, const)
            load(xt[:], mem[0:P, :], xt_full)
            for dst, src in ((ident[:], ident_d), (gn[:], gains), (snk[:], sink)):
                load(dst, src, const)
            for i in range(2, 4):
                sp.wait_ge(x_lo.sem, 2 * (i - 1))
                load(xraw[:, i % 2, :], memT[:, i * 512:(i + 1) * 512], xraw_full[i % 2])
                sp.wait_ge(w_lo.sem, 2 * (i - 1))
                load(raw[:, i % 2, :], w_kv[:, i * 1024:(i + 1) * 1024], raw_full[i % 2])
            sp.wait_ge(x_sq.sem, 1)
            load(xt[:], mem[P:2 * P, :], xt_full)
            for k in range(2):
                sp.wait_ge(x_lo.sem, 2 * (k + 3))
                load(xraw[:, k, :], xT[0, :, k * 512:(k + 1) * 512], xraw_full[k])
            for u in range(2):
                sp.wait_ge(w_lo.sem, 2 * (u + 3))
                load(raw[:, u, :], w_unit(u), raw_full[u])
            for k in range(2, KT):
                if k % 2 == 0:
                    sp.wait_ge(x_sq.sem, 1 + k // 2)
                    load(xt[:], x[(k // 2 - 1) * P:(k // 2) * P, :], xt_full)
                sp.wait_ge(x_lo.sem, KT + k - 1)
                load(xraw[:, k % 2, :], xT[0, :, k * 512:(k + 1) * 512], xraw_full[k % 2])
                if k == 3:
                    for i in range(3):
                        load(bias[:, i], alibi[:, i], const)
            sp.wait_ge(x_sq.sem, 5)
            load(xt[:], x[3 * P:4 * P, :], xt_full)

            with sp.Fori(0, BLOCKS) as b:
                for u in range(UNITS):
                    sp.wait_ge(w_lo.sem, w_lo.at(b, 2 * u + 2))
                    sp.dma_start(raw[:, u % 2, :], w_unit((u + 2) % UNITS)).then_inc(raw_full[u % 2].sem, 16)
                    if u >= 22 and (u - 22) < KT:
                        k = u - 22
                        sp.wait_ge(x_lo.sem, x_lo.at(b, k - 1))
                        sp.dma_start(xraw[:, k % 2, :], xT[bass.ds(b + 1, 1), :, k * 512:(k + 1) * 512].rearrange(
                            "a p n -> (a p) n")).then_inc(xraw_full[k % 2].sem, 16)
                    if u in (20, 24, 26, 28):
                        t = (20, 24, 26, 28).index(u)
                        sp.wait_ge(x_sq.sem, x_sq.at(b, t))
                        sp.dma_start(xt[:], x[bass.ds(b * BLOCK + (BLOCK + t * P), P), :]).then_inc(xt_full.sem, 16)
                    if u in (23, 30):
                        o = (23, 30).index(u)
                        sp.wait_ge(stored.sem, stored.at(b, 64 * o))
                        sp.dma_start(res[:], x[bass.ds(b * BLOCK, BLOCK), o * 512:(o + 1) * 512].rearrange(
                            "(t p) n -> p t n", p=P)).then_inc(res_full.sem, 16)
                    if u in (28, 31):
                        o = (28, 31).index(u)
                        for t in range(TILES):
                            sp.wait_ge(o_done.sem, o_done.at(b, 4 * o + t + 1))
                            sp.dma_start(out[bass.ds(b * BLOCK + t * P, P), o * 512:(o + 1) * 512],
                                         res[:, t, :]).then_inc(stored.sem, 16)
            sp.wait_ge(stored.sem, stored.at(BLOCKS, 0))
            for i in range(2):
                sp.wait_ge(raw_full[i].sem, raw_full[i].at(BLOCKS, 16))

        @block.gpsimd
        def _(pool):
            pool.memset(zeros[:], 0.0).then_inc(ready.sem, 1)
            pool.memset(half[:], -0.5).then_inc(ready.sem, 1)
            pool.memset(kTe[:, 0, 1, :], 0.0).then_inc(ready.sem, 1)
            pool.memset(ones[:], 1.0).then_inc(ready.sem, 1)
            pool.sem_inc(stored.sem, 64)
            pool.sem_inc(o_done.sem, 4)

            def power(out_, in_):
                return pool.tensor_tensor(out_, in_, half[:, 0:in_.shape[1]], ALU.pow)

            def x_power(col, val):
                pool.wait_ge(x_var.sem, val)
                power(xr[:, col:col + 1], xvar[:, col:col + 1]).then_inc(x_r.sem, 1)

            x_power(4, 1)
            x_power(5, 2)
            for t in range(2):
                pool.wait_ge(u_var.sem, t + 1)
                power(ur[:, t, :], uvar[:, t, :]).then_inc(u_r.sem, 1)
            for t in range(TILES):
                x_power(t, 3 + t)

            with pool.Fori(0, BLOCKS) as b:
                for n in range(STEPS):
                    for u in stage(2 * n, 1) + stage(2 * n + 1, 1):
                        pool.wait_ge(p_rinv.sem, p_rinv.at(b, u + 1))
                        segs = 2 if u < MEM_UNITS else 4
                        pv = ps[:, u % 3, :].rearrange("p (s k) -> p s k", s=segs)
                        pool.tensor_tensor(pv, pv, rinv[:, u % 3, 0:segs].unsqueeze(2).to_broadcast(
                            [P, segs, 512 // segs]), ALU.mult).then_inc(p_norm.sem, 1)
                    for s, e in enumerate(A_ENDS):
                        if n in (e + 1, e + 2):
                            for t in (2 * (n - e - 1), 2 * (n - e - 1) + 1):
                                pool.wait_ge(u_var.sem, u_var.at(b, 4 * s + t + 1))
                                power(ur[:, t, :], uvar[:, t, :]).then_inc(u_r.sem, 1)
                    if n in X_SQUARE:
                        k = X_SQUARE[n]
                        x_power(k, x_var.at(b, k + 1))

        @block.scalar
        def _(act):
            def hi_of_chunk(slot, half_, wait):
                ring = wait[0]
                act.wait_ge(wait[1].sem, wait[2])
                if wait[3] is not None:
                    act.wait_ge(wait[3][0].sem, wait[3][1])
                act.activation(ws[:, ring, 0, :], raw[:, slot, half_ * 512:(half_ + 1) * 512],
                               ACT.Copy).then_inc(w_hi.sem, 1)

            def x_square(col, val, before):
                act.wait_ge(xt_full.sem, val)
                if before is not None:
                    act.wait_ge(x_sq.sem, before)
                act.activation(tmp[:].rearrange("p a b -> p (a b)"), xt[:], ACT.Square, scale=D_MODEL ** -0.5,
                               accum_out=xss[:, col:col + 1]).then_inc(x_sq.sem, 1)

            def x_hi_part(k, cols, src, g, wait, value):
                act.wait_ge(wait.sem, value)
                return act.activation(xnT[:, 0, k, cols], src, ACT.Copy, scale=gx[:, g, k:k + 1])

            act.wait_ge(const.sem, 64)
            for k in range(KT):
                x_hi_part(k, slice(0, 256), xraw[:, (k // 2) % 2, (k % 2) * 256:(k % 2 + 1) * 256], 1,
                          xraw_full[(k // 2) % 2], 16 * (k // 4 + 1)).then_inc(x_hi.sem, 1)
                c = k
                hi_of_chunk((c // 2) % 2, c % 2, (c % WRING, raw_full[(c // 2) % 2], 16 * (c // 4 + 1),
                                                  (step_done, c - 3) if c >= 4 else None))
                if k in (1, 5):
                    x_square(4 + k // 4, 16 * (k // 4 + 1), k // 4 if k > 4 else None)
            for t in range(2):
                act.wait_ge(acc_done.sem, t + 1)
                act.wait_ge(x_r.sem, 2)
                act.activation(u_tok[:, t, :], acc[t][:], ACT.Copy, scale=xr[:, 4 + t:5 + t]).then_inc(u_raw.sem, 1)
                act.wait_ge(u_raw.sem, t + 1)
                act.activation(tmp[:, t, :], u_tok[:, t, :], ACT.Square, scale=HD ** -0.5).then_inc(u_sq.sem, 1)
                act.activation(mv[:, t, 0, :], u_tok[:, t, 256:512], ACT.Copy).then_inc(v_hi.sem, 1)
            for k in range(KT):
                x_hi_part(k, slice(0, 512), xraw[:, k % 2, :], 0, xraw_full[k % 2],
                          32 + 16 * (k // 2 + 1)).then_inc(x_hi.sem, 1)
                if k < LEAD:
                    c = 8 + k
                    hi_of_chunk((c // 2) % 2, c % 2, (c % WRING, raw_full[(c // 2) % 2], 48, (step_done, c - 3)))
                if k == 1:
                    act.wait_ge(u_ss.sem, 2)
                if k % 2 == 1:
                    x_square(k // 2, 32 + 16 * (k // 2 + 1), 2 + k // 2)

            def exponentials(b, u):
                r = u % 3
                segs = 2 if u < MEM_UNITS else 4
                w = 512 // segs
                act.wait_ge(sc_neg.sem, sc_neg.at(b, u + 1))
                for s in range(segs):
                    last = act.activation(ps[:, r, s * w:(s + 1) * w], ps[:, r, s * w:(s + 1) * w], ACT.Exp,
                                          bias=nmax[:, r, s:s + 1], scale=-1.0, accum_out=den[:, r, s:s + 1])
                if u >= MEM_UNITS:
                    act.wait_ge(sk_arg.sem, sk_arg.at(b, u - MEM_UNITS + 1))
                    last = act.activation(esk[:, r, :], dsk[:, r, :], ACT.Exp)
                last.then_inc(p_exp.sem, 1)

            with act.Fori(0, BLOCKS) as b:
                for n in range(STEPS):
                    c = n + LEAD
                    slot = (c // 2) % 2
                    hi_of_chunk(slot, c % 2, (c % WRING, raw_full[slot], raw_full[slot].at(b, 16 * (c // 4 + 1)),
                                              step_over(b, c - WRING)))
                    if n in X_SQUARE:
                        k = X_SQUARE[n]
                        x_square(k, xt_full.at(b, 16 * (k + 1)), x_sq.at(b, k))
                    if n in X_SPLIT:
                        k = X_SPLIT[n]
                        x_hi_part(k, slice(0, 512), xraw[:, k % 2, :], 0, xraw_full[k % 2],
                                  xraw_full[k % 2].at(b, 16 * (k // 2 + 1))).then_inc(x_hi.sem, 1)
                    for half_ in range(2):
                        key = (n, 2 * half_ + 1)
                        if key in TP_HI:
                            i = TP_AT[key][1]
                            act.wait_ge(tp_full.sem, tp_full.at(b, TP_INDEX[key] + 1))
                            act.activation(pT[:, i % 2, 0, :], tp[:], ACT.Copy).then_inc(tp_hi.sem, 1)
                        for u in stage(2 * n + half_, 0):
                            exponentials(b, u)
                    for s, e in enumerate(A_ENDS):
                        if n in (e + 1, e + 2):
                            for t in (2 * (n - e - 1), 2 * (n - e - 1) + 1):
                                if s == 0:
                                    act.activation(vO[:, t, 0, :], u_tok[:, t, P:2 * P], ACT.Copy).then_inc(v_hi.sem, 1)
                                act.wait_ge(u_ss.sem, u_ss.at(b, 4 * s + t - 1))
                                act.activation(tmp[:, t % 2, :], u_tok[:, t, :], ACT.Square,
                                               scale=HD ** -0.5).then_inc(u_sq.sem, 1)
                    if O_0 - 2 <= n < STEPS - 2:
                        i = n + 2 - O_0
                        over = step_over(b, n - 1)
                        act.wait_ge(y_prod.sem, y_prod.at(b, min(i, YT - 1) + 1))
                        act.wait_ge(over[0].sem, over[1])
                        act.activation(ys[:, i % YRING, 0, :], y[:, i % YT, :], ACT.Copy).then_inc(y_hi.sem, 1)
                    if n in A_ENDS:
                        s = A_ENDS.index(n)
                        for t in range(TILES):
                            act.wait_ge(acc_done.sem, acc_done.at(b, 4 * s + t + 1))
                            act.activation(u_tok[:, t, :], acc[t][:], ACT.Copy,
                                           scale=xr[:, t:t + 1]).then_inc(u_raw.sem, 1)
                        act.wait_ge(u_raw.sem, u_raw.at(b, 4 * s + 4))
                    if n in G_ENDS:
                        k0, kn = G_ENDS[n]
                        for t in range(kn):
                            act.wait_ge(g_raw.sem, g_raw.at(b, k0 + t + 1))
                            if k0 + t >= 2:
                                act.wait_ge(g_done.sem, g_done.at(b, k0 + t - 1))
                            act.activation(tmp[:, t % 2, :], gate[:, k0 + t, :], ACT.Tanh, scale=0.5).then_inc(g_th.sem, 1)

        @block.vector
        def _(dve):
            dve.wait_ge(const.sem, 64)
            dve.wait_ge(ready.sem, 4)
            dve.tensor_scalar(nsnk[:], snk[:], -1.0, None, ALU.mult).then_inc(ready.sem, 1)
            dve.tensor_scalar(gn[:, 0:2], gn[:, 0:2], HD ** -0.5, None, ALU.mult).then_inc(ready.sem, 1)
            dve.tensor_copy(vE[64:128, 0, :, :].rearrange("p a b -> p (a b)"), zeros[64:128, :]).then_inc(halo.sem, 1)
            dve.wait_ge(ready.sem, 6)

            def lo_of_chunk(slot, half_, ring, val):
                dve.wait_ge(w_hi.sem, val)
                dve.tensor_tensor(ws[:, ring, 1, :], raw[:, slot, half_ * 512:(half_ + 1) * 512],
                                  ws[:, ring, 0, :].bitcast(F32), ALU.subtract).then_inc(w_lo.sem, 1)

            def x_mean(col, val):
                dve.wait_ge(x_sq.sem, val)
                dve.tensor_scalar(xvar[:, col:col + 1], xss[:, col:col + 1], EPS, None, ALU.add).then_inc(x_var.sem, 1)

            def x_lo_part(k, cols, src, g, val):
                dve.wait_ge(x_hi.sem, val)
                dve.scalar_tensor_tensor(out=xnT[:, 1, k, cols], in0=src, scalar=gx[:, g, k:k + 1],
                                         in1=xnT[:, 0, k, cols].bitcast(F32), op0=ALU.mult,
                                         op1=ALU.subtract).then_inc(x_lo.sem, 1)

            def head_squares(t, sq_val, ss_val):
                dve.wait_ge(u_sq.sem, sq_val)
                dve.tensor_reduce(uss[:, t, :], tmp[:, t % 2, :].rearrange("p (h d) -> p h d", d=HD), AX.X,
                                  ALU.add).then_inc(u_ss.sem, 1)
                dve.wait_ge(u_ss.sem, ss_val)
                dve.tensor_scalar(uvar[:, t, :], uss[:, t, :], EPS, None, ALU.add).then_inc(u_var.sem, 1)

            def scale_heads(t, h0, h1):
                v = u_tok[:, t, h0 * HD:h1 * HD].rearrange("p (h d) -> p h d", d=HD)
                return dve.tensor_tensor(v, v, ur[:, t, h0:h1].unsqueeze(2).to_broadcast([P, h1 - h0, HD]), ALU.mult)

            for k in range(KT):
                x_lo_part(k, slice(0, 256), xraw[:, (k // 2) % 2, (k % 2) * 256:(k % 2 + 1) * 256], 1, k + 1)
                c = k
                lo_of_chunk((c // 2) % 2, c % 2, c % WRING, c + 1)
                if k in (2, 6):
                    x_mean(4 + k // 4, k // 4 + 1)
            for t in range(2):
                head_squares(t, t + 1, t + 1)
            for t in range(2):
                dve.wait_ge(u_r.sem, t + 1)
                scale_heads(t, 0, 4).then_inc(u_n.sem, 1)
                dve.wait_ge(v_hi.sem, t + 1)
                dve.tensor_tensor(mv[:, t, 1, :], u_tok[:, t, 256:512], mv[:, t, 0, :].bitcast(F32),
                                  ALU.subtract).then_inc(v_lo.sem, 1)
            for k in range(KT):
                x_lo_part(k, slice(0, 512), xraw[:, k % 2, :], 0, KT + k + 1)
                if k < LEAD:
                    c = 8 + k
                    lo_of_chunk((c // 2) % 2, c % 2, c % WRING, c + 1)
                if k % 2 == 1:
                    x_mean(k // 2, 2 + k // 2 + 1)
                if k in (2, 3):
                    t = k - 2
                    dve.wait_ge(tp_full.sem, t + 1)
                    dve.tensor_scalar(mkT[:, :, t * P:(t + 1) * P], tp[:, 0:256].rearrange("p (k t) -> p k t", k=2),
                                      gn[:, 3:4], None, ALU.mult).then_inc(tp_free.sem, 1)

            def scores(b, u):
                r = u % 3
                if u < MEM_UNITS:
                    for s in range(2):
                        last = dve.tensor_tensor_reduce(
                            ps[:, r, s * 256:(s + 1) * 256], sc[u % 2][:, s * 256:(s + 1) * 256], zeros[:], -1.0, BIG,
                            ALU.add, ALU.min, nmax[:, r, s:s + 1])
                    last.then_inc(sc_neg.sem, 1)
                    return
                c, g = (u - MEM_UNITS) // 2, (u - MEM_UNITS) % 2
                table = 2 if c == 0 else c % 2
                for s in range(4):
                    pair = 4 * g + s
                    last = dve.tensor_tensor_reduce(
                        ps[:, r, s * P:(s + 1) * P], sc[u % 2][:, s * P:(s + 1) * P], bias[:, table, pair, :], -1.0,
                        nsnk[:, pair:pair + 1], ALU.add, ALU.min, nmax[:, r, s:s + 1])
                last.then_inc(sc_neg.sem, 1)
                dve.wait_ge(sc_neg.sem, sc_neg.at(b, u + 1))
                dve.tensor_tensor(dsk[:, r, :], nmax[:, r, :], nsnk[:, 4 * g:4 * g + 4],
                                  ALU.subtract).then_inc(sk_arg.sem, 1)

            def denominators(b, u):
                r = u % 3
                segs = 2 if u < MEM_UNITS else 4
                dve.wait_ge(p_exp.sem, p_exp.at(b, u + 1))
                if u >= MEM_UNITS:
                    dve.tensor_tensor(dtot[:, r, :], den[:, r, :], esk[:, r, :], ALU.add).then_inc(d_sum.sem, 1)
                    dve.wait_ge(d_sum.sem, d_sum.at(b, u - MEM_UNITS + 1))
                total = den if u < MEM_UNITS else dtot
                dve.reciprocal(rinv[:, r, 0:segs], total[:, r, 0:segs]).then_inc(p_rinv.sem, 1)

            def tp_event(b, n, place):
                key = (n, place)
                if key not in TP_INDEX:
                    return
                kind, s, t = TP_AT[key]
                if kind == "p":
                    dve.wait_ge(tp_hi.sem, tp_hi.at(b, TP_HI[key] + 1))
                    dve.tensor_tensor(pT[:, s % 2, 1, :], tp[:], pT[:, s % 2, 0, :].bitcast(F32),
                                      ALU.subtract).then_inc(tp_free.sem, 1)
                    return
                dve.wait_ge(tp_full.sem, tp_full.at(b, TP_INDEX[key] + 1))
                if kind == "r":
                    dve.tensor_copy(rbc[:], tp[:]).then_inc(tp_free.sem, 1)
                elif s == 0:
                    dve.tensor_scalar(kTo[:, t, :], tp[:, 0:P], gn[:, 2:3], None, ALU.mult)
                    dve.tensor_scalar(kTe[:, t, 0, :], tp[:, 0:CHUNK], gn[:, 2:3], None, ALU.mult)
                    if t == TILES - 1:
                        dve.wait_ge(halo.sem, halo.at(b, 0))
                    dve.tensor_scalar(kTe[:, t + 1, 1, :], tp[:, CHUNK:P], gn[:, 2:3], None, ALU.mult)
                    dve.tensor_scalar(mqT[:, :, t * P:(t + 1) * P], tp[:, P:3 * P].rearrange("p (k t) -> p k t", k=2),
                                      gn[:, 1:2], None, ALU.mult).then_inc(tp_free.sem, 1)
                else:
                    j0 = 4 * (s - 1)
                    for cc in range(2):
                        last = dve.tensor_scalar(qT[:, 2 * t + cc, j0:j0 + 4, :],
                                                 tp[:].rearrange("p (j c q) -> p j c q", c=2, q=CHUNK)[:, :, cc, :],
                                                 gn[:, 0:1], None, ALU.mult)
                    last.then_inc(tp_free.sem, 1)

            def y_out(b, u):
                dve.wait_ge(y_full.sem, y_full.at(b, u + 1))
                if u < MEM_UNITS:
                    t, a = u // 2, u % 2
                    dve.tensor_copy(y[0:64, a, t * P:(t + 1) * P], yb[0:64, 0:P])
                    dve.tensor_copy(y[64:128, a, t * P:(t + 1) * P], yb[64:128, P:2 * P]).then_inc(y_free.sem, 1)
                else:
                    c, g = (u - MEM_UNITS) // 2, (u - MEM_UNITS) % 2
                    h = slice(64 * g, 64 * g + 64)
                    dve.tensor_copy(y[h, 2:10, c * CHUNK:(c + 1) * CHUNK],
                                    yb[h, :].rearrange("p (j q) -> p j q", q=CHUNK)).then_inc(y_free.sem, 1)

            def attention(b, n, half_):
                hs = 2 * n + half_
                for u in stage(hs, 0):
                    dve.wait_ge(sc_full.sem, sc_full.at(b, u + 1))
                for u in stage(hs, 1):
                    denominators(b, u)
                if half_ == 0:
                    c = n + LEAD
                    lo_of_chunk((c // 2) % 2, c % 2, c % WRING, w_hi.at(b, c + 1))
                for u in stage(hs, 0):
                    scores(b, u)
                tp_event(b, n, 2 * half_)
                tp_event(b, n, 2 * half_ + 1)
                for u in stage(hs, PV_LAG):
                    y_out(b, u)

            dve.wait_ge(const.sem, N_CONST)
            with dve.Fori(0, BLOCKS) as b:
                for n in range(STEPS):
                    if n == 1:
                        dve.wait_ge(x_r.sem, x_r.at(b, 0))
                        for t in range(TILES):
                            last = dve.tensor_scalar(tmp[:, 0, t * P:(t + 1) * P], ident[:], xr[:, t:t + 1], None,
                                                     ALU.mult)
                        last.then_inc(r_diag.sem, 1)
                    attention(b, n, 0)
                    for s, e in enumerate(A_ENDS):
                        if n in (e + 1, e + 2):
                            for t in (2 * (n - e - 1), 2 * (n - e - 1) + 1):
                                head_squares(t, u_sq.at(b, 4 * s + t + 1), u_ss.at(b, 4 * s + t + 1))
                                if s == 0:
                                    dve.wait_ge(v_hi.sem, v_hi.at(b, t + 1))
                                    dve.tensor_tensor(vO[:, t, 1, :], u_tok[:, t, P:2 * P],
                                                      vO[:, t, 0, :].bitcast(F32), ALU.subtract).then_inc(v_lo.sem, 1)
                        if n in (e + 2, e + 3):
                            for t in (2 * (n - e - 2), 2 * (n - e - 2) + 1):
                                dve.wait_ge(u_r.sem, u_r.at(b, 4 * s + t + 1))
                                if s == 0:
                                    scale_heads(t, 0, 2)
                                    scale_heads(t, 4, 8).then_inc(u_n.sem, 1)
                                else:
                                    scale_heads(t, 0, 8).then_inc(u_n.sem, 1)
                    if n == A_ENDS[0] + 3:
                        dve.wait_ge(v_lo.sem, v_lo.at(b, TILES))
                        dve.wait_ge(halo.sem, halo.at(b, 0))
                        dve.tensor_copy(vE[0:64, 0:TILES].rearrange("p t a d -> p (t a d)"),
                                        vO[0:64].rearrange("p t a d -> p (t a d)").bitcast(F32))
                        dve.tensor_copy(vE[64:128, 1:].rearrange("p t a d -> p (t a d)"),
                                        vO[64:128].rearrange("p t a d -> p (t a d)").bitcast(F32)).then_inc(v_even.sem, 1)
                    if n in X_SQUARE:
                        k = X_SQUARE[n]
                        x_mean(k, x_sq.at(b, k + 1))
                    if n in X_SPLIT:
                        k = X_SPLIT[n]
                        x_lo_part(k, slice(0, 512), xraw[:, k % 2, :], 0, x_hi.at(b, k + 1))
                    attention(b, n, 1)
                    if n in Y_GATE:
                        k = Y_GATE[n]
                        dve.wait_ge(y_free.sem, y_free.at(b, MEM_UNITS if k < 2 else N_UNITS))
                        dve.wait_ge(g_done.sem, g_done.at(b, 2 if k < 2 else YT))
                        dve.scalar_tensor_tensor(out=y[:, k, :], in0=gate[:, k, :], scalar=0.5, in1=y[:, k, :],
                                                 op0=ALU.mult, op1=ALU.mult).then_inc(y_prod.sem, 1)
                    if O_0 - 2 <= n < STEPS - 2:
                        i = n + 2 - O_0
                        dve.wait_ge(y_hi.sem, y_hi.at(b, i + 1))
                        dve.tensor_tensor(ys[:, i % YRING, 1, :], y[:, i % YT, :], ys[:, i % YRING, 0, :].bitcast(F32),
                                          ALU.subtract).then_inc(y_lo.sem, 1)
                    if n in G_ENDS:
                        k0, kn = G_ENDS[n]
                        for t in range(kn):
                            dve.wait_ge(acc_done.sem, acc_done.at(b, 12 + k0 + t + 1))
                            dve.tensor_tensor(gate[:, k0 + t, :], acc[t][:], rbc[:], ALU.mult).then_inc(g_raw.sem, 1)
                        for t in range(kn):
                            dve.wait_ge(g_th.sem, g_th.at(b, k0 + t + 1))
                            dve.scalar_tensor_tensor(out=gate[:, k0 + t, :], in0=tmp[:, t % 2, :], scalar=1.0,
                                                     in1=gate[:, k0 + t, :], op0=ALU.add, op1=ALU.mult).then_inc(g_done.sem, 1)
                    if n in O_ENDS:
                        o = O_ENDS[n]
                        dve.wait_ge(res_full.sem, res_full.at(b, 16 * (o + 1)))
                        for t in range(TILES):
                            dve.wait_ge(acc_done.sem, acc_done.at(b, 22 + 4 * o + t + 1))
                            dve.tensor_tensor(res[:, t, :], acc[t][:], res[:, t, :], ALU.add).then_inc(o_done.sem, 1)
                    if n == 48:
                        dve.wait_ge(y_full.sem, y_full.at(b, N_UNITS))
                        dve.tensor_copy(bias[:, 2], bias[:, 0])
                        dve.tensor_copy(vE[64:128, 0], vE[64:128, TILES].bitcast(F32))
                        dve.tensor_copy(kTe[:, 0, 1, :], kTe[:, TILES, 1, :]).then_inc(halo.sem, 1)

        @block.tensor
        def _(pe):
            PASSES = ((0, 0), (0, 1), (1, 0))

            for k in range(KT):
                pe.wait_ge(w_lo.sem, k + 1)
                pe.wait_ge(x_lo.sem, k + 1)
                for t in range(2):
                    for i, (a, w) in enumerate(PASSES):
                        last = pe.matmul(acc[t][:], xnT[:, a, k, t * P:(t + 1) * P], ws[:, k % WRING, w, :],
                                         start=(k == 0 and i == 0), stop=(k == KT - 1 and i == 2))
                    if k == KT - 1:
                        last.then_inc(acc_done.sem, 1)
                if k < KT - 1:
                    last.then_inc(step_done.sem, 1)
            pe.wait_ge(const.sem, 64)
            for t in range(2):
                pe.wait_ge(u_n.sem, t + 1)
                if t:
                    pe.wait_ge(tp_free.sem, t)
                for j in range(2):
                    last = pe.transpose(tp[:, j * P:(j + 1) * P], u_tok[:, t, j * P:(j + 1) * P], ident[:])
                last.then_inc(tp_full.sem, 1)
            def qk(b, u):
                s = sc[u % 2]
                if u >= 2:
                    pe.wait_ge(sc_neg.sem, sc_neg.at(b, u - 1))
                if u == MEM_UNITS:
                    pe.wait_ge(halo.sem, halo.at(b, 0))
                if u < MEM_UNITS:
                    t, a = u // 2, u % 2
                    pe.wait_ge(tp_free.sem, tp_free.at(b, TP_OF["q", 0, t] + 1))
                    h = slice(64 * a, 64 * a + 64)
                    for hp in range(2):
                        last = pe.matmul(s[:, hp * 256:(hp + 1) * 256], mqT[h, hp, t * P:(t + 1) * P], mkT[h, hp, :],
                                         start=True, stop=True)
                else:
                    c, g = (u - MEM_UNITS) // 2, (u - MEM_UNITS) % 2
                    t = c // 2
                    pe.wait_ge(tp_free.sem, tp_free.at(b, TP_OF["q", 2, t] + 1))
                    h = slice(64 * g, 64 * g + 64)
                    keys = kTo[h, t, :] if c % 2 else kTe[h, t, :, :].rearrange("p a b -> p (a b)")
                    for p in range(4):
                        last = pe.matmul(s[:, p * P:(p + 1) * P],
                                         qT[h, c, 2 * p:2 * p + 2, :].rearrange("p a b -> p (a b)"), keys,
                                         start=True, stop=True)
                last.then_inc(sc_full.sem, 1)

            def p_transposes(b, u):
                pe.wait_ge(p_norm.sem, p_norm.at(b, u + 1))
                for j in range(4):
                    i = (j % 2) * 2 + j // 2 if u < MEM_UNITS else j
                    last = pe.transpose(tp[:, j * P:(j + 1) * P], ps[:, u % 3, i * P:(i + 1) * P], ident[:])
                return last

            def pv(b, u):
                r = u % 2
                pe.wait_ge(tp_free.sem, tp_free.at(b, TP_OF["p", u, 0] + 1))
                if u > 0:
                    pe.wait_ge(y_free.sem, y_free.at(b, u))
                if u < MEM_UNITS:
                    a = u % 2
                    for kt in range(2):
                        for i, (v, p) in enumerate(PASSES):
                            last = pe.matmul(yb[:, 0:256], mv[:, kt, v, a * P:(a + 1) * P],
                                             pT[:, r, p, kt * 256:(kt + 1) * 256],
                                             start=(kt == 0 and i == 0), stop=(kt == 1 and i == 2))
                else:
                    c = (u - MEM_UNITS) // 2
                    v_ = vO if c % 2 else vE
                    pe.wait_ge(v_even.sem, v_even.at(b, 1))
                    for i, (v, p) in enumerate(PASSES):
                        last = pe.matmul(yb[:], v_[:, c // 2, v, :], pT[:, r, p, :], start=(i == 0), stop=(i == 2))
                last.then_inc(y_full.sem, 1)

            def tp_event(b, n, place):
                key = (n, place)
                if key not in TP_INDEX:
                    return
                kind, i, h = TP_AT[key]
                free = tp_free.at(b, TP_INDEX[key])
                pe.wait_ge(tp_free.sem, free)
                if kind == "r":
                    pe.wait_ge(r_diag.sem, r_diag.at(b, 1))
                    pe.matmul(tp[:], ones[:], tmp[:, 0, :], start=True, stop=True).then_inc(tp_full.sem, 1)
                    return
                if kind == "p":
                    p_transposes(b, i).then_inc(tp_full.sem, 1)
                    return
                s, t = i, h
                pe.wait_ge(u_n.sem, u_n.at(b, 4 * s + t + 1))
                cols = (0, 2, 3) if s == 0 else (0, 1, 2, 3)
                for j, cblk in enumerate(cols):
                    last = pe.transpose(tp[:, j * P:(j + 1) * P], u_tok[:, t, cblk * P:(cblk + 1) * P], ident[:])
                last.then_inc(tp_full.sem, 1)

            def group(b, n, t):
                ring = n % WRING
                if n < G_0:
                    k, K = n % 8, KT
                    return [(xnT[:, a, k, t * P:(t + 1) * P], ws[:, ring, w, :]) for a, w in PASSES], k == 0, k == K - 1
                if n < G_1:
                    m = n - G_0
                    return [(ws[:, ring, w, kk * 256 + t * P:kk * 256 + (t + 1) * P], xnT[:, a, 2 * m + kk, :])
                            for kk in range(2) for w, a in PASSES], m == 0, m == 3
                if n < O_0:
                    k = (n - G_1) % 8
                    return [(ws[:, ring, w, t * P:(t + 1) * P], xnT[:, a, k, :]) for w, a in PASSES], k == 0, k == 7
                k = (n - O_0) % YT
                yr = (n - O_0) % YRING
                return [(ys[:, yr, a, t * P:(t + 1) * P], ws[:, ring, w, :]) for a, w in PASSES], k == 0, k == YT - 1

            with pe.Fori(0, BLOCKS) as b:
                for n in range(STEPS):
                    pe.wait_ge(w_lo.sem, w_lo.at(b, n + 1))
                    if n >= O_0:
                        pe.wait_ge(y_lo.sem, y_lo.at(b, n - O_0 + 1))
                    if n < KT:
                        pe.wait_ge(x_lo.sem, x_lo.at(b, n + 1 - KT))
                    tiles = 2 if G_0 <= n < G_1 else 4
                    for t in range(4):
                        if t % 2 == 0:
                            for u in stage(2 * n + t // 2, 0):
                                qk(b, u)
                        tp_event(b, n, t)
                        if t % 2 == 1:
                            for u in stage(2 * n + t // 2, PV_LAG):
                                pv(b, u)
                        if t >= tiles:
                            continue
                        ops, first, final = group(b, n, t)
                        if first:
                            who, how_many = bank_free(n, t)
                            cnt = {"o_done": o_done, "u_raw": u_raw, "g_raw": g_raw}[who]
                            pe.wait_ge(cnt.sem, cnt.at(b, how_many))
                        for i, (lhs, rhs) in enumerate(ops):
                            last = pe.matmul(acc[t][:], lhs, rhs, start=(first and i == 0),
                                             stop=(final and i == len(ops) - 1))
                        if final:
                            last.then_inc(acc_done.sem, 1)
                    if not final:
                        last.then_inc(step_done.sem, 1)


def head_columns():
    import numpy as np

    d = np.arange(HD)
    mem_cols = [N_HEADS * HD + h * HD + d for h in (0, 2, 1, 3)]
    win_cols = [h * HD + d for j in range(PAIRS) for h in (j, PAIRS + j)]
    return np.concatenate(mem_cols), np.concatenate(win_cols)


def alibi_table():
    import numpy as np

    slopes = np.float32(2.0) ** (np.float32(-8.0) * np.arange(1, N_HEADS + 1, dtype=np.float32) / np.float32(N_HEADS))
    q = np.arange(CHUNK)[:, None]
    k = np.arange(2 * CHUNK)[None, :]
    dist = np.abs(q - k + CHUNK).astype(np.float32)
    t = np.zeros((P, 3, PAIRS, P), np.float32)
    for pair in range(PAIRS):
        for a in range(2):
            rows = slice(a * CHUNK, (a + 1) * CHUNK)
            odd = -slopes[2 * pair + a] * dist
            even = np.concatenate([odd[:, CHUNK:], odd[:, :CHUNK]], axis=1)
            t[rows, 0, pair] = even
            t[rows, 1, pair] = odd
            t[rows, 2, pair] = even
            t[rows, 2, pair, CHUNK:] = -1e30
    return t


def kernel(**inputs):
    import numpy as np
    import concourse.bacc as bacc
    from concourse.bass_utils import run_bass_kernel_spmd

    f32 = np.float32
    x = np.ascontiguousarray(inputs["x"]).reshape(SEQ, D_MODEL)
    mem = np.ascontiguousarray(inputs["mem"]).reshape(N_MEM, D_MODEL)
    w_in = np.asarray(inputs["a_w_in"])[0]
    w_out = np.asarray(inputs["w_out"])[0]
    mem_cols, win_cols = head_columns()
    kv0 = N_HEADS * HD
    mq0 = kv0 + 2 * KV_HEADS * HD
    g0 = mq0 + MEM_HEADS * HD
    w_kv = np.asarray(inputs["mem_w_kv"])
    gate_cols = g0 + np.concatenate([mem_cols, win_cols])

    def chunks(w):
        k, n = w.shape
        return w.reshape(k // P, P, n).transpose(1, 0, 2).reshape(P, -1)

    slices = [w_in[:, kv0:g0], w_in[:, win_cols[:512]], w_in[:, win_cols[512:]],
              w_in[:, gate_cols[256:768]], w_in[:, gate_cols[768:]]]
    w_rows = w_out[np.concatenate([mem_cols, win_cols])]
    gains = [inputs["a_q_norm_g"][0], inputs["mem_q_norm_g"][0], inputs["a_k_norm_g"][0], inputs["mem_k_norm_g"]]
    arrays = {
        "x": np.concatenate([x, np.zeros((BLOCK, D_MODEL), f32)]),
        "xT": np.concatenate([x.reshape(BLOCKS, BLOCK, KT, P).transpose(0, 3, 2, 1).reshape(BLOCKS, P, -1),
                              np.zeros((1, P, KT * BLOCK), f32)]),
        "mem": mem,
        "memT": mem.reshape(N_MEM, KT, P).transpose(2, 1, 0).reshape(P, -1),
        "w_in": np.stack([chunks(w) for w in slices]),
        "w_gate0": chunks(w_in[:, gate_cols[:256]]),
        "w_out": np.stack([chunks(w_rows[:, :512]), chunks(w_rows[:, 512:])]),
        "w_kv": chunks(np.concatenate([w_kv[:, :256], w_kv[:, mem_cols - kv0 + 256]], axis=1)),
        "norm_gains": np.concatenate([np.asarray(inputs[g]).reshape(KT, P).T for g in ("norm_g", "mem_norm_g")], axis=1),
        "gains": np.stack([np.tile(np.asarray(g), 2) for g in gains], axis=1),
        "sink": np.repeat(np.asarray(inputs["a_sink"])[0].reshape(PAIRS, 2).T, CHUNK, axis=0),
        "ident": np.eye(P, dtype=f32),
        "alibi": alibi_table(),
    }
    nc = bacc.Bacc("TRN2", target_bir_lowering=False, num_devices=1)
    feeds, args = {}, []
    for name, a in arrays.items():
        a = np.ascontiguousarray(a)
        feeds[f"in_{name}"] = a
        args.append(nc.dram_tensor(f"in_{name}", a.shape, F32, kind="ExternalInput").ap())
    args.append(nc.dram_tensor("out_0", (SEQ, D_MODEL), F32, kind="ExternalOutput").ap())
    encoder_layer(nc, *args)
    r = run_bass_kernel_spmd(nc, [feeds], core_ids=[0])
    return r.results[0]["out_0"].reshape(1, SEQ, D_MODEL)
```

```python
from contextlib import ExitStack

import concourse.bass as bass
from concourse import mybir

F32 = mybir.dt.float32
F32R = mybir.dt.float32r
ALU = mybir.AluOpType
ACT = mybir.ActivationFunctionType
AX = mybir.AxisListType

P = 128
D_MODEL, SEQ, N_MEM = 1024, 2048, 256
HD = 64
CHUNK = 64
N_HEADS, KV_HEADS, MEM_HEADS = 16, 2, 4
EPS = 1e-6
BLOCK = 512
BLOCKS = SEQ // BLOCK
TILES = BLOCK // P
KT = D_MODEL // P
YT = (N_HEADS + MEM_HEADS) // 2
PAIRS = N_HEADS // 2
CPB = BLOCK // CHUNK
BIG = 3.0e38
NEG = -1e30
PASSES = ((0, 0), (0, 1), (1, 0))

A_KV, A_Q0, A_Q1 = 0, 8, 16
G_0, G_1, G_2 = 24, 28, 36
O_0, O_1 = 44, 54
STEPS = 64
LEAD = 3
WRING = 4
YRING = 3
UNITS = STEPS // 2
A_ENDS = (7, 15, 23)
G_ENDS = {27: (0, 2), 35: (2, 4), 43: (6, 4)}
O_ENDS = {53: 0, 63: 1}
FINALS = (*A_ENDS, *G_ENDS, *O_ENDS)
PRO_CHUNKS = KT

MEM_UNITS = 8
WIN_UNITS = 16
N_UNITS = MEM_UNITS + WIN_UNITS
T_LAG, PV_LAG = 2, 3
MEM_START, WIN_START, WIN_SPAN = 4 * 13, 4 * 28, 60
SLOTS = {}
for i in range(MEM_UNITS + PV_LAG):
    SLOTS[MEM_START + 4 * i] = (0, MEM_UNITS, i)
for i in range(WIN_UNITS + PV_LAG):
    SLOTS[WIN_START + round(i * WIN_SPAN / (WIN_UNITS + PV_LAG - 1))] = (MEM_UNITS, WIN_UNITS, i)


def stage(q, lag):
    if q not in SLOTS:
        return []
    first, units, i = SLOTS[q]
    return [first + i - lag] if 0 <= i - lag < units else []


def outputs_of(q):
    return [u for u in stage(q, PV_LAG) if u in PV_UNITS]


MEM_UNIT = ((0, 0), (1, 0), (1, 1), (0, 1), (2, 0), (3, 0), (3, 1), (2, 1))
PT_SLOT = [(0, 1, 2, 1)[u % 4] if u < MEM_UNITS else u % 2 for u in range(N_UNITS)]
PV_UNITS = [u for u in range(N_UNITS) if u >= MEM_UNITS or u % 2 == 1]
MEM_PVS = MEM_UNITS // 2

TP_AT = {(23, 1): ("r", 0, 0)}
for s, e in enumerate(A_ENDS):
    for t in range(TILES):
        q = 4 * (e + 4) + 2 * t
        TP_AT[divmod(q + 1 if outputs_of(q - 2) else q, 4)] = ("q", s, t)
for q in SLOTS:
    for u in stage(q, T_LAG):
        TP_AT[divmod(q + 1, 4)] = ("p", u, 0)
TP_ORDER = sorted(TP_AT)
TP_INDEX = {key: i for i, key in enumerate(TP_ORDER)}
TP_OF = {TP_AT[key]: TP_INDEX[key] for key in TP_ORDER}
TP_HI = {}
for key in TP_ORDER:
    if TP_AT[key][0] == "p":
        TP_HI[key] = len(TP_HI)
PRO_TP = 2
TURNS = sorted([(4 * n + t, "tp") for n, t in TP_AT] + [(q + 2, "y") for q in SLOTS if outputs_of(q)])
TURN_OF = {turn: i for i, turn in enumerate(TURNS)}
BANKS = 3
assert len(TURNS) % BANKS == 0 and len({q for q, _ in TURNS}) == len(TURNS)
X_SPLIT = {46 + 2 * k: k for k in range(KT)}
X_SQUARE = {2: 0, 3: 1, 4: 2, 5: 3}
R_DIAG = 22
HALO = 48
SILU = {(e + 3 + t // 2, 1 + 2 * (t % 2)): (k0 + t, t) for e, (k0, kn) in G_ENDS.items() for t in range(kn)}
V_EVEN = 21
Y_GATE = {38: 0, 39: 1, **{42 + k: k for k in range(2, YT)}}
POOL_LO = range(32, 48)


def banks(n):
    return sum(2 if e == 27 else 4 for e in FINALS if e <= n)


def bank_free(n, t):
    return {A_KV: ("o_done", t - 3), A_Q0: ("u_raw", t + 1), A_Q1: ("u_raw", 4 + t + 1), G_0: ("u_raw", 8 + t + 1),
            G_1: ("g_raw", t + 1) if t < 2 else ("u_raw", 8 + t + 1), G_2: ("g_raw", 2 + t + 1),
            O_0: ("g_raw", 6 + t + 1), O_1: ("o_done", t + 1)}[n]


class Count:
    def __init__(self, sem, per, base):
        self.sem, self.per, self.base = sem, per, base

    def at(self, turn, n):
        return turn * self.per + (self.base + n)


def encoder_layer(nc, x, xT, mem, memT, w_in, w_gate0, w_out, w_kv, norm_gains, gains, sink, ident_d, alibi, out):
    ctx = ExitStack()
    with ctx:
        def sb(name, shape, dt=F32):
            return ctx.enter_context(nc.sbuf_tensor(name, shape, dt))

        def count(name, per, base):
            return Count(ctx.enter_context(nc.semaphore(name)), per, base)

        raw = sb("raw", [P, 2, 1024])
        ws = sb("w_split", [P, WRING, 2, 512], F32R)
        xnT = sb("xnT", [P, 2, KT, BLOCK], F32R)
        xraw = sb("xraw", [P, 2, 512])
        gx = sb("gx", [P, 2, KT])
        u_tok = sb("u_tok", [P, TILES, 512])
        tmp = sb("tmp", [P, 2, 512])
        qT = sb("qT", [P, CPB, PAIRS, CHUNK])
        kTo = sb("kT_odd", [P, TILES, P])
        kTe = sb("kT_even", [P, TILES + 1, 2, CHUNK])
        vO = sb("v_odd", [P, TILES, KV_HEADS, 2 * HD], F32R)
        vE = sb("v_even", [P, TILES + 1, KV_HEADS, 2 * HD], F32R)
        mk = sb("mk", [P, MEM_HEADS, 2, N_MEM], F32R)
        mv = sb("mv", [P, 2, MEM_HEADS, 2 * HD], F32R)
        ps = sb("p_score", [P, 3, 512])
        pT = sb("pT", [P, 3, 2, 512], F32R)
        y = sb("y", [P, YT, BLOCK])
        gate = sb("gate", [P, YT, BLOCK])
        ys = sb("y_split", [P, YRING, 2, BLOCK], F32R)
        res = sb("res", [P, TILES, 512])
        bias = sb("alibi_sb", [P, 3, PAIRS, P])
        ident = sb("ident", [P, P])
        zeros = sb("zeros", [P, 1])
        gn = sb("gn", [P, 4])
        snk = sb("snk", [P, PAIRS])
        nsnk = sb("nsnk", [P, PAIRS])
        half = sb("half", [P, 8])
        ones = sb("ones", [P, P])
        rbc = sb("rbc", [P, BLOCK])
        xss = sb("xss", [P, 6])
        xvar = sb("xvar", [P, 6])
        xr = sb("xr", [P, 6])
        uss = sb("uss", [P, TILES, 8])
        uvar = sb("uvar", [P, TILES, 8])
        ur = sb("ur", [P, TILES, 8])
        nmax = sb("nmax", [P, 3, 4])
        dsk = sb("dsk", [P, 3, 4])
        esk = sb("esk", [P, 3, 4])
        den = sb("den", [P, 3, 4])
        dtot = sb("dtot", [P, 3, 4])
        rinv = sb("rinv", [P, 3, 4])

        acc = [ctx.enter_context(nc.psum_tensor(f"acc{i}", [P, 512], F32)) for i in range(TILES)]
        turn = [ctx.enter_context(nc.psum_tensor(f"turn{i}", [P, 512], F32)) for i in range(BANKS)]
        sc = ctx.enter_context(nc.psum_tensor("sc", [P, 512], F32))

        raw_full = [count(f"raw_full{i}", 16 * UNITS // 2, 16) for i in range(2)]
        w_hi = count("w_hi", STEPS, PRO_CHUNKS)
        w_lo = count("w_lo", STEPS - len(POOL_LO), PRO_CHUNKS)
        w_lo_pool = count("w_lo_pool", len(POOL_LO), 0)
        step_done = count("step_done", STEPS - len(FINALS), PRO_CHUNKS - 2)
        acc_done = count("acc_done", 30, 4)
        nat_full = [count(f"nat_full{i}", 16, 16) for i in range(TILES)]
        xraw_full = [count(f"xraw_full{i}", 64, 0) for i in range(2)]
        xT_full = [count(f"xT_full{i}", 0, 16) for i in range(4)]
        memT_full = [count(f"memT_full{i}", 0, 16) for i in range(4)]
        mem_full = [count(f"mem_full{i}", 0, 16) for i in range(2)]
        kv_full = [count(f"kv_full{i}", 0, 16) for i in range(2)]
        x_hi = count("x_hi", KT, 2 * KT)
        x_lo = count("x_lo", KT, 2 * KT)
        x_sq = count("x_sq", 4, 2)
        x_var = count("x_var", 4, 2)
        x_r = count("x_r", 4, 2)
        r_diag = count("r_diag", 1, 0)
        u_raw = count("u_raw", 12, 2)
        u_sq = count("u_sq", 12, 2)
        u_ss = count("u_ss", 12, 2)
        u_var = count("u_var", 12, 2)
        u_r = count("u_r", 12, 2)
        u_n = count("u_n", 12, 2)
        v_hi = count("v_hi", 4, 2)
        v_lo = count("v_lo", 4, 2)
        v_even = count("v_even", 1, 0)
        halo = count("halo", 1, 1)
        tp_full = count("tp_full", len(TP_ORDER), PRO_TP)
        tp_hi = count("tp_hi", len(TP_HI), 0)
        mk_hi = count("mk_hi", 0, 2)
        mk_both = count("mk_both", 0, 2)
        mq_hi = count("mq_hi", TILES, 0)
        tp_free = count("tp_free", len(TP_ORDER), PRO_TP)
        sc_full = count("sc_full", N_UNITS, 0)
        sc_neg = count("sc_neg", N_UNITS, 0)
        sk_arg = count("sk_arg", WIN_UNITS, 0)
        p_exp = count("p_exp", N_UNITS, 0)
        d_sum = count("d_sum", WIN_UNITS, 0)
        p_rinv = count("p_rinv", N_UNITS, 0)
        p_norm = count("p_norm", N_UNITS, 0)
        y_full = count("y_full", len(PV_UNITS), 0)
        y_half = count("y_half", len(PV_UNITS), 0)
        y_free = count("y_free", len(PV_UNITS), 0)
        g_raw = count("g_raw", YT, 0)
        g_th = count("g_th", YT, 0)
        g_done = count("g_done", YT, 0)
        y_prod = count("y_prod", YT, 0)
        y_hi = count("y_hi", 2 * YT, 0)
        y_lo = count("y_lo", 2 * YT, 0)
        res_full = count("res_full", 32, 0)
        o_done = count("o_done", 8, 4)
        stored = count("stored", 128, 64)
        gx_full = count("gx_full", 0, 16)
        bias_set = count("bias_set", 0, 4)
        const = count("const", 0, 64)
        ready = count("ready", 0, 0)

        def step_over(b, n):
            if n in FINALS or n == -1:
                return acc_done, acc_done.at(b, banks(n))
            return step_done, step_done.at(b, sum(m not in FINALS for m in range(n + 1)))

        def lo_done(b, c):
            turns, c = divmod(c, STEPS)
            who = w_lo_pool if c in POOL_LO else w_lo
            return who, who.at(b, turns * who.per + sum((m in POOL_LO) == (c in POOL_LO) for m in range(c + 1)))

        def tp_bank(key):
            return turn[TURN_OF[4 * key[0] + key[1], "tp"] % BANKS]

        Y_TURNS = [i for i, (_, kind) in enumerate(TURNS) if kind == "y"]

        def y_bank(u):
            return turn[Y_TURNS[PV_UNITS.index(u)] % BANKS]

        def bank_read(b, i):
            if i < BANKS:
                return tp_free, tp_free.at(b, 0)
            q, kind = TURNS[i - BANKS]
            who = tp_free if kind == "tp" else y_free
            return who, who.at(b, sum(k == kind for _, k in TURNS[:i - BANKS + 1]))

        block = ctx.enter_context(nc.Block())

        def w_unit(u):
            if u < 12:
                return w_in[u // 4, :, (u % 4) * 1024:(u % 4 + 1) * 1024]
            if u < 14:
                return w_gate0[:, (u - 12) * 1024:(u - 11) * 1024]
            if u < 22:
                return w_in[3 + (u - 14) // 4, :, ((u - 14) % 4) * 1024:((u - 14) % 4 + 1) * 1024]
            return w_out[(u - 22) // 5, :, ((u - 22) % 5) * 1024:((u - 22) % 5 + 1) * 1024]

        slope_dist = rbc[:, 0:PAIRS + 2 * P]

        def x_tok(t):
            return y[:, 2 * t:2 * t + 2, :].rearrange("p a b -> p (a b)")

        def mem_tok(t):
            return (u_tok[:, 2:4, :], y[:, 8:10, :])[t].rearrange("p a b -> p (a b)")

        def mem_feat(k):
            return (xraw[:, k // 2, :] if k < 4 else gate[:, 6 + k // 2, :])[:, (k % 2) * 256:(k % 2 + 1) * 256]

        def kv_unit(u):
            return raw[:, u, :] if u < 2 else res[:, 2 * (u - 2):2 * (u - 1), :].rearrange("p a b -> p (a b)")

        def kv_chunk(c):
            return kv_unit(c // 2)[:, (c % 2) * 512:(c % 2 + 1) * 512]

        def kv_landed(c):
            return raw_full[c // 2] if c < 4 else kv_full[c // 2 - 2]

        mq = ys[:, 0:2].rearrange("p a b n -> p (a b) n")

        def head_pair(bank, a, cols):
            return bank[64 * a:64 * a + 64, cols].rearrange("p (k t) -> p k t", k=2)

        y_lows = xraw[:, 0, :]

        def heads(ap):
            return ap.rearrange("p (h d) -> p h d", d=HD)

        def raw_chunk(c):
            return raw[:, (c // 2) % 2, (c % 2) * 512:(c % 2 + 1) * 512]

        @block.sync
        def _(sp):
            def load(dst, src, signal):
                sp.dma_start(dst, src).then_inc(signal.sem, 16)

            for i in range(2):
                load(xraw[:, i, :], memT[:, i * 512:(i + 1) * 512], memT_full[i])
                load(raw[:, i, :], w_kv[:, i * 1024:(i + 1) * 1024], raw_full[i])
                if i == 0:
                    load(gx[:].rearrange("p a b -> p (a b)"), norm_gains, gx_full)
                load(gate[:, 8 + i, :], memT[:, (2 + i) * 512:(3 + i) * 512], memT_full[2 + i])
            for i in range(2):
                load(mem_tok(i), mem[i * P:(i + 1) * P, :], mem_full[i])
                load(kv_unit(2 + i), w_kv[:, (2 + i) * 1024:(3 + i) * 1024], kv_full[i])
            for dst, src in ((ident[:], ident_d), (gn[:], gains), (snk[:], sink), (slope_dist, alibi)):
                load(dst, src, const)
            for i in range(4):
                load(gate[:, 2 * i:2 * i + 2, :].rearrange("p a b -> p (a b)"),
                     xT[0, :, i * 1024:(i + 1) * 1024], xT_full[i])
                if i < 2:
                    sp.wait_ge(w_lo.sem, 2 * i + 2)
                    load(raw[:, i, :], w_unit(i), raw_full[i])
            for t in range(TILES):
                load(x_tok(t), x[t * P:(t + 1) * P, :], nat_full[t])

            with sp.Fori(0, BLOCKS) as b:
                for u in range(UNITS):
                    split = lo_done(b, 2 * u + 1)
                    sp.wait_ge(split[0].sem, split[1])
                    sp.dma_start(raw[:, u % 2, :], w_unit((u + 2) % UNITS)).then_inc(raw_full[u % 2].sem, 16)
                    if u >= 22 and (u - 22) < KT:
                        k = u - 22
                        sp.wait_ge(x_lo.sem, x_lo.at(b, k - 1))
                        if k == 0:
                            sp.wait_ge(y_free.sem, y_free.at(b, len(PV_UNITS)))
                        sp.dma_start(xraw[:, k % 2, :], xT[bass.ds(b + 1, 1), :, k * 512:(k + 1) * 512].rearrange(
                            "a p n -> (a p) n")).then_inc(xraw_full[k % 2].sem, 16)
                    if u in (23, 30):
                        o = (23, 30).index(u)
                        sp.wait_ge(stored.sem, stored.at(b, 64 * o))
                        sp.dma_start(res[:], x[bass.ds(b * BLOCK, BLOCK), o * 512:(o + 1) * 512].rearrange(
                            "(t p) n -> p t n", p=P)).then_inc(res_full.sem, 16)
                    if u == UNITS - 1:
                        sp.wait_ge(y_lo.sem, y_lo.at(b, 2 * YT))
                        for t in range(TILES):
                            sp.dma_start(x_tok(t), x[bass.ds(b * BLOCK + (BLOCK + t * P), P), :]).then_inc(
                                nat_full[t].sem, 16)
                    if u in (28, 31):
                        o = (28, 31).index(u)
                        for t in range(TILES):
                            sp.wait_ge(o_done.sem, o_done.at(b, 4 * o + t + 1))
                            sp.dma_start(out[bass.ds(b * BLOCK + t * P, P), o * 512:(o + 1) * 512],
                                         res[:, t, :]).then_inc(stored.sem, 16)
            sp.wait_ge(stored.sem, stored.at(BLOCKS, 0))
            for i in range(2):
                sp.wait_ge(raw_full[i].sem, raw_full[i].at(BLOCKS, 16))
            for t in range(TILES):
                sp.wait_ge(nat_full[t].sem, nat_full[t].at(BLOCKS, 0))

        @block.gpsimd
        def _(pool):
            pool.memset(zeros[:], 0.0).then_inc(ready.sem, 1)
            pool.memset(half[:], -0.5).then_inc(ready.sem, 1)
            pool.memset(kTe[:, 0, 1, :], 0.0).then_inc(ready.sem, 1)
            pool.memset(ones[:], 1.0).then_inc(ready.sem, 1)
            pool.sem_inc(stored.sem, 64)
            pool.sem_inc(o_done.sem, 4)

            def power(out_, in_):
                return pool.tensor_tensor(out_, in_, half[:, 0:in_.shape[1]], ALU.pow)

            def x_power(col, val):
                pool.wait_ge(x_var.sem, val)
                power(xr[:, col:col + 1], xvar[:, col:col + 1]).then_inc(x_r.sem, 1)

            pool.wait_ge(ready.sem, 4)
            x_power(4, 1)
            x_power(5, 2)
            for t in range(2):
                pool.wait_ge(u_var.sem, t + 1)
                power(ur[:, t, 0:4], uvar[:, t, 0:4]).then_inc(u_r.sem, 1)

            pool.wait_ge(const.sem, 64)
            for table, which in ((0, 0), (1, 1), (2, 0)):
                pool.tensor_tensor(bias[:, table],
                                   slope_dist[:, PAIRS + which * P:PAIRS + (which + 1) * P].unsqueeze(1).to_broadcast(
                                       [P, PAIRS, P]),
                                   slope_dist[:, 0:PAIRS].unsqueeze(2).to_broadcast([P, PAIRS, P]),
                                   ALU.mult).then_inc(bias_set.sem, 1)
            pool.wait_ge(bias_set.sem, 3)
            pool.memset(bias[:, 2, :, CHUNK:], NEG).then_inc(bias_set.sem, 1)

            pool.wait_ge(bias_set.sem, 4)
            for t in range(2):
                pool.wait_ge(tp_free.sem, t + 1)
                if t:
                    pool.wait_ge(mk_both.sem, t)
                cols = slice(t * P, (t + 1) * P)
                pool.tensor_copy(mk[64:128, :, :, cols].rearrange("p h a n -> p (h a) n"),
                                 mk[0:64, :, :, cols].rearrange("p h a n -> p (h a) n").bitcast(F32)).then_inc(
                                     mk_both.sem, 1)
            pool.wait_ge(mk_both.sem, 2)

            with pool.Fori(0, BLOCKS) as b:
                for n in range(STEPS):
                    for t in range(4):
                        for u in stage(4 * n + t, 1):
                            pool.wait_ge(p_rinv.sem, p_rinv.at(b, u + 1))
                            segs = 2 if u < MEM_UNITS else 4
                            pv = ps[:, u % 3, :].rearrange("p (s k) -> p s k", s=segs)
                            pool.tensor_tensor(pv, pv, rinv[:, u % 3, 0:segs].unsqueeze(2).to_broadcast(
                                [P, segs, 512 // segs]), ALU.mult).then_inc(p_norm.sem, 1)
                        if t == 0 and n + LEAD in POOL_LO:
                            c = n + LEAD
                            pool.wait_ge(w_hi.sem, w_hi.at(b, c + 1))
                            pool.tensor_tensor(ws[:, c % WRING, 1, :], raw_chunk(c), ws[:, c % WRING, 0, :].bitcast(F32),
                                               ALU.subtract).then_inc(w_lo_pool.sem, 1)
                    for s, e in enumerate(A_ENDS):
                        if n in (e + 1, e + 2):
                            for t in (2 * (n - e - 1), 2 * (n - e - 1) + 1):
                                pool.wait_ge(u_var.sem, u_var.at(b, 4 * s + t + 1))
                                power(ur[:, t, :], uvar[:, t, :]).then_inc(u_r.sem, 1)
                    if n in X_SQUARE:
                        k = X_SQUARE[n]
                        x_power(k, x_var.at(b, k + 1))
                    if n in Y_GATE:
                        k = Y_GATE[n]
                        pool.wait_ge(y_free.sem, y_free.at(b, MEM_PVS if k < 2 else len(PV_UNITS)))
                        pool.wait_ge(g_done.sem, g_done.at(b, k + 1))
                        pool.tensor_tensor(y[:, k, :], y[:, k, :], gate[:, k, :], ALU.mult).then_inc(y_prod.sem, 1)

        @block.scalar
        def _(act):
            def hi_of_chunk(c, src, landed, how_many, over):
                act.wait_ge(landed.sem, how_many)
                if over is not None:
                    act.wait_ge(over[0].sem, over[1])
                act.activation(ws[:, c % WRING, 0, :], src, ACT.Copy).then_inc(w_hi.sem, 1)

            def x_square(col, src, landed, how_many, before):
                act.wait_ge(landed.sem, how_many)
                if before is not None:
                    act.wait_ge(x_sq.sem, before)
                act.activation(tmp[:].rearrange("p a b -> p (a b)"), src, ACT.Square, scale=D_MODEL ** -0.5,
                               accum_out=xss[:, col:col + 1]).then_inc(x_sq.sem, 1)

            def x_hi_part(k, cols, src, g, wait, value):
                act.wait_ge(wait.sem, value)
                return act.activation(xnT[:, 0, k, cols], src, ACT.Copy, scale=gx[:, g, k:k + 1])

            def kv_hi(c):
                over = None if c < 4 else (acc_done, 2) if c == 7 else (step_done, c - 3)
                hi_of_chunk(c, kv_chunk(c), kv_landed(c), 16, over)

            act.wait_ge(gx_full.sem, 16)
            for c in range(4):
                for k in (2 * c, 2 * c + 1):
                    x_hi_part(k, slice(0, 256), mem_feat(k), 1, memT_full[c], 16).then_inc(x_hi.sem, 1)
                kv_hi(c)
            for t in range(2):
                x_square(4 + t, mem_tok(t), mem_full[t], 16, t or None)
            kv_hi(4)
            kv_hi(5)
            act.wait_ge(x_r.sem, 2)
            for t in range(2):
                act.wait_ge(acc_done.sem, t + 1)
                act.activation(u_tok[:, t, 0:256], acc[t][:, 0:256], ACT.Copy, scale=xr[:, 4 + t:5 + t]).then_inc(u_raw.sem, 1)
                act.wait_ge(u_raw.sem, t + 1)
                act.activation(tmp[:, t, 0:256], u_tok[:, t, 0:256], ACT.Square, scale=HD ** -0.5).then_inc(u_sq.sem, 1)
            kv_hi(6)
            kv_hi(7)
            for k in range(KT):
                if k % 2 == 0:
                    over = (acc_done, 4) if k == 6 else (step_done, 4 + k // 2)
                    act.wait_ge(over[0].sem, over[1])
                x_hi_part(k, slice(0, 512), gate[:, k, :], 0, xT_full[k // 2], 16).then_inc(x_hi.sem, 1)
                if k < LEAD:
                    hi_of_chunk(k, raw_chunk(k), raw_full[k // 2], 32, (step_done, k + 4))
                if k == 0:
                    for t in range(2):
                        act.wait_ge(acc_done.sem, 3 + t)
                        act.activation(mv[:, t, :, 0:HD], heads(acc[2 + t][:, 0:256]), ACT.Copy,
                                       scale=xr[:, 4 + t:5 + t]).then_inc(v_hi.sem, 1)

            for t in range(2):
                act.wait_ge(tp_full.sem, t + 1)
                act.wait_ge(const.sem, 64)
                for a in range(2):
                    last = act.activation(mk[0:64, a::2, 0, t * P:(t + 1) * P], head_pair(turn[t], a, slice(0, 256)),
                                          ACT.Copy, scale=gn[64 * a:64 * a + 64, 3:4])
                last.then_inc(mk_hi.sem, 1)

            def exponentials(b, u):
                r = u % 3
                segs = 2 if u < MEM_UNITS else 4
                w = 512 // segs
                act.wait_ge(sc_neg.sem, sc_neg.at(b, u + 1))
                for s in range(segs):
                    last = act.activation(ps[:, r, s * w:(s + 1) * w], ps[:, r, s * w:(s + 1) * w], ACT.Exp,
                                          bias=nmax[:, r, s:s + 1], scale=-1.0, accum_out=den[:, r, s:s + 1])
                if u >= MEM_UNITS:
                    act.wait_ge(sk_arg.sem, sk_arg.at(b, u - MEM_UNITS + 1))
                    last = act.activation(esk[:, r, :], dsk[:, r, :], ACT.Exp)
                last.then_inc(p_exp.sem, 1)

            def y_low(b, u):
                index = PV_UNITS.index(u)
                yb = y_bank(u)
                act.wait_ge(y_full.sem, y_full.at(b, index + 1))
                if index > 0:
                    act.wait_ge(y_free.sem, y_free.at(b, index if u < MEM_UNITS else max(MEM_PVS, index - 1)))
                if u < MEM_UNITS:
                    for hp in range(2):
                        last = act.activation(y_lows[64 * hp:64 * hp + 64, 0:256],
                                              yb[64:128, hp * 256:(hp + 1) * 256], ACT.Copy)
                else:
                    g = (u - MEM_UNITS) % 2
                    last = act.activation(y_lows[64 * g:64 * g + 64, :], yb[64:128, :], ACT.Copy)
                last.then_inc(y_half.sem, 1)

            with act.Fori(0, BLOCKS) as b:
                for n in range(STEPS):
                    for u in outputs_of(4 * n - 3):
                        y_low(b, u)
                    c = n + LEAD
                    landed = raw_full[(c // 2) % 2]
                    hi_of_chunk(c, raw_chunk(c), landed, landed.at(b, 16 * (c // 4 + 1)), step_over(b, c - WRING))
                    if n in X_SQUARE:
                        k = X_SQUARE[n]
                        if k == 0:
                            act.wait_ge(u_ss.sem, u_ss.at(b, 0))
                        x_square(k, x_tok(k), nat_full[k], nat_full[k].at(b, 0), x_sq.at(b, k))
                    if n in X_SPLIT:
                        k = X_SPLIT[n]
                        x_hi_part(k, slice(0, 512), xraw[:, k % 2, :], 0, xraw_full[k % 2],
                                  xraw_full[k % 2].at(b, 16 * (k // 2 + 1))).then_inc(x_hi.sem, 1)
                    for t in range(4):
                        for u in outputs_of(4 * n + t - 3) if t > 0 else []:
                            y_low(b, u)
                        key = (n, t)
                        if key in TP_HI:
                            i = TP_AT[key][1]
                            act.wait_ge(tp_full.sem, tp_full.at(b, TP_INDEX[key] + 1))
                            act.activation(pT[:, PT_SLOT[i], 0, :], tp_bank(key)[:], ACT.Copy).then_inc(tp_hi.sem, 1)
                        if key in TP_AT and TP_AT[key][:2] == ("q", 0):
                            tile = TP_AT[key][2]
                            act.wait_ge(tp_full.sem, tp_full.at(b, TP_INDEX[key] + 1))
                            act.activation(kTo[:, tile, :], tp_bank(key)[:, 0:P], ACT.Copy, scale=gn[:, 2:3])
                            for a in range(2):
                                last = act.activation(mq[0:64, a::2, tile * P:(tile + 1) * P],
                                                      head_pair(tp_bank(key), a, slice(P, 3 * P)), ACT.Copy,
                                                      scale=gn[64 * a:64 * a + 64, 1:2])
                            last.then_inc(mq_hi.sem, 1)
                        for u in stage(4 * n + t - 1, 0):
                            exponentials(b, u)
                        for s, e in enumerate(A_ENDS):
                            if n in (e + 1, e + 2) and t % 2 == 0:
                                tile = 2 * (n - e - 1) + t // 2
                                if s == 0:
                                    act.activation(vO[:, tile, :, 0:HD], heads(u_tok[:, tile, P:2 * P]),
                                                   ACT.Copy).then_inc(v_hi.sem, 1)
                                act.wait_ge(u_ss.sem, u_ss.at(b, 4 * s + tile - 1))
                                act.activation(tmp[:, tile % 2, :], u_tok[:, tile, :], ACT.Square,
                                               scale=HD ** -0.5).then_inc(u_sq.sem, 1)
                        if n - 1 in G_ENDS and t < G_ENDS[n - 1][1]:
                            k = G_ENDS[n - 1][0] + t
                            act.wait_ge(g_raw.sem, g_raw.at(b, k + 1))
                            act.activation(u_tok[:, t, :] if k >= 2 else tmp[:, t, :], gate[:, k, :],
                                           ACT.Tanh).then_inc(g_th.sem, 1)
                        if n in A_ENDS:
                            s = A_ENDS.index(n)
                            if (s, t) == (0, 0):
                                act.wait_ge(x_r.sem, x_r.at(b, TILES))
                            act.wait_ge(acc_done.sem, acc_done.at(b, 4 * s + t + 1))
                            act.activation(u_tok[:, t, :], acc[t][:], ACT.Copy,
                                           scale=xr[:, t:t + 1]).then_inc(u_raw.sem, 1)
                    if O_0 - 2 <= n < STEPS - 2:
                        i = n + 2 - O_0
                        over = step_over(b, n - 1)
                        act.wait_ge(y_prod.sem, y_prod.at(b, min(i, YT - 1) + 1))
                        act.wait_ge(over[0].sem, over[1])
                        act.activation(ys[:, i % YRING, 0, :], y[:, i % YT, :], ACT.Copy).then_inc(y_hi.sem, 1)
                    if n in A_ENDS:
                        act.wait_ge(u_raw.sem, u_raw.at(b, 4 * A_ENDS.index(n) + 4))

        @block.vector
        def _(dve):
            def lo_of_chunk(c, src, val):
                dve.wait_ge(w_hi.sem, val)
                dve.tensor_tensor(ws[:, c % WRING, 1, :], src, ws[:, c % WRING, 0, :].bitcast(F32),
                                  ALU.subtract).then_inc(w_lo.sem, 1)

            def x_mean(col, val):
                dve.wait_ge(x_sq.sem, val)
                dve.tensor_scalar(xvar[:, col:col + 1], xss[:, col:col + 1], EPS, None, ALU.add).then_inc(x_var.sem, 1)

            def x_lo_part(k, cols, src, g, val):
                dve.wait_ge(x_hi.sem, val)
                dve.scalar_tensor_tensor(out=xnT[:, 1, k, cols], in0=src, scalar=gx[:, g, k:k + 1],
                                         in1=xnT[:, 0, k, cols].bitcast(F32), op0=ALU.mult,
                                         op1=ALU.subtract).then_inc(x_lo.sem, 1)

            def head_squares(t, heads, sq_val, ss_val):
                dve.wait_ge(u_sq.sem, sq_val)
                dve.tensor_reduce(uss[:, t, 0:heads], tmp[:, t % 2, 0:heads * HD].rearrange("p (h d) -> p h d", d=HD),
                                  AX.X, ALU.add).then_inc(u_ss.sem, 1)
                dve.wait_ge(u_ss.sem, ss_val)
                dve.tensor_scalar(uvar[:, t, 0:heads], uss[:, t, 0:heads], EPS, None, ALU.add).then_inc(u_var.sem, 1)

            def scale_heads(t, h0, h1):
                v = u_tok[:, t, h0 * HD:h1 * HD].rearrange("p (h d) -> p h d", d=HD)
                return dve.tensor_tensor(v, v, ur[:, t, h0:h1].unsqueeze(2).to_broadcast([P, h1 - h0, HD]), ALU.mult)

            def kv_lo(c):
                lo_of_chunk(c, kv_chunk(c), c + 1)

            for c in range(4):
                for k in (2 * c, 2 * c + 1):
                    x_lo_part(k, slice(0, 256), mem_feat(k), 1, k + 1)
                kv_lo(c)
            for t in range(2):
                x_mean(4 + t, t + 1)
            kv_lo(4)
            kv_lo(5)
            dve.wait_ge(const.sem, 64)
            dve.wait_ge(ready.sem, 4)
            dve.tensor_scalar(nsnk[:], snk[:], -1.0, None, ALU.mult).then_inc(ready.sem, 1)
            dve.tensor_scalar(gn[:, 0:2], gn[:, 0:2], HD ** -0.5, None, ALU.mult).then_inc(ready.sem, 1)
            dve.tensor_copy(vE[64:128, 0, :, :].rearrange("p a b -> p (a b)"),
                            zeros[64:128, :].to_broadcast([64, 256])).then_inc(halo.sem, 1)
            dve.wait_ge(ready.sem, 6)

            for t in range(2):
                head_squares(t, 4, t + 1, t + 1)
            kv_lo(6)
            kv_lo(7)
            for t in range(2):
                dve.wait_ge(u_r.sem, t + 1)
                scale_heads(t, 0, 4).then_inc(u_n.sem, 1)
            for k in range(KT):
                x_lo_part(k, slice(0, 512), gate[:, k, :], 0, KT + k + 1)
                if k < LEAD:
                    lo_of_chunk(k, raw_chunk(k), PRO_CHUNKS + k + 1)
                if k == 0:
                    for t in range(2):
                        dve.wait_ge(v_hi.sem, t + 1)
                        dve.scalar_tensor_tensor(out=mv[:, t, :, HD:], in0=heads(acc[2 + t][:, 0:256]),
                                                 scalar=xr[:, 4 + t:5 + t], in1=mv[:, t, :, 0:HD].bitcast(F32), op0=ALU.mult,
                                                 op1=ALU.subtract).then_inc(v_lo.sem, 1)
            for t in range(2):
                dve.wait_ge(mk_hi.sem, t + 1)
                for a in range(2):
                    last = dve.scalar_tensor_tensor(out=mk[0:64, a::2, 1, t * P:(t + 1) * P],
                                                    in0=head_pair(turn[t], a, slice(0, 256)), scalar=gn[0:64, 3:4],
                                                    in1=mk[0:64, a::2, 0, t * P:(t + 1) * P].bitcast(F32),
                                                    op0=ALU.mult, op1=ALU.subtract)
                last.then_inc(tp_free.sem, 1)

            def scores(b, u):
                r = u % 3
                if u < MEM_UNITS:
                    for s in range(2):
                        last = dve.tensor_tensor_reduce(
                            ps[:, r, s * 256:(s + 1) * 256], sc[:, s * 256:(s + 1) * 256],
                            zeros[:].to_broadcast([P, 256]), -1.0, BIG,
                            ALU.add, ALU.min, nmax[:, r, s:s + 1])
                    last.then_inc(sc_neg.sem, 1)
                    return
                c, g = (u - MEM_UNITS) // 2, (u - MEM_UNITS) % 2
                table = 2 if c == 0 else c % 2
                for s in range(4):
                    pair = 4 * g + s
                    last = dve.tensor_tensor_reduce(
                        ps[:, r, s * P:(s + 1) * P], sc[:, s * P:(s + 1) * P], bias[:, table, pair, :], -1.0,
                        nsnk[:, pair:pair + 1], ALU.add, ALU.min, nmax[:, r, s:s + 1])
                last.then_inc(sc_neg.sem, 1)
                dve.wait_ge(sc_neg.sem, sc_neg.at(b, u + 1))
                dve.tensor_tensor(dsk[:, r, :], nmax[:, r, :], nsnk[:, 4 * g:4 * g + 4],
                                  ALU.subtract).then_inc(sk_arg.sem, 1)

            def denominators(b, u):
                r = u % 3
                segs = 2 if u < MEM_UNITS else 4
                dve.wait_ge(p_exp.sem, p_exp.at(b, u + 1))
                if u >= MEM_UNITS:
                    dve.tensor_tensor(dtot[:, r, :], den[:, r, :], esk[:, r, :], ALU.add).then_inc(d_sum.sem, 1)
                    dve.wait_ge(d_sum.sem, d_sum.at(b, u - MEM_UNITS + 1))
                total = den if u < MEM_UNITS else dtot
                dve.reciprocal(rinv[:, r, 0:segs], total[:, r, 0:segs]).then_inc(p_rinv.sem, 1)

            def tp_event(b, n, place):
                key = (n, place)
                if key not in TP_INDEX:
                    return
                kind, s, t = TP_AT[key]
                bank = tp_bank(key)
                if kind == "p":
                    dve.wait_ge(tp_hi.sem, tp_hi.at(b, TP_HI[key] + 1))
                    dve.tensor_tensor(pT[:, PT_SLOT[s], 1, :], bank[:], pT[:, PT_SLOT[s], 0, :].bitcast(F32),
                                      ALU.subtract).then_inc(tp_free.sem, 1)
                    return
                if (kind, s) == ("q", 0):
                    dve.wait_ge(mq_hi.sem, mq_hi.at(b, t + 1))
                else:
                    dve.wait_ge(tp_full.sem, tp_full.at(b, TP_INDEX[key] + 1))
                if kind == "r":
                    dve.tensor_scalar(rbc[:], bank[:], 0.5, None, ALU.mult).then_inc(tp_free.sem, 1)
                elif s == 0:
                    if t == TILES - 1:
                        dve.wait_ge(halo.sem, halo.at(b, 0))
                    dve.tensor_scalar(kTe[:].rearrange("p t a q -> p (t a) q")[:, 2 * t:2 * t + 4:3, :],
                                      bank[:, 0:P].rearrange("p (a q) -> p a q", a=2), gn[:, 2:3], None, ALU.mult)
                    for a in range(2):
                        last = dve.scalar_tensor_tensor(out=mq[64:128, a::2, t * P:(t + 1) * P],
                                                        in0=head_pair(bank, a, slice(P, 3 * P)), scalar=gn[0:64, 1:2],
                                                        in1=mq[0:64, a::2, t * P:(t + 1) * P].bitcast(F32),
                                                        op0=ALU.mult, op1=ALU.subtract)
                    last.then_inc(tp_free.sem, 1)
                else:
                    j0 = 4 * (s - 1)
                    last = dve.tensor_scalar(qT[:, 2 * t:2 * t + 2, j0:j0 + 4, :].rearrange("p c j q -> p j c q"),
                                             bank[:].rearrange("p (j c q) -> p j c q", c=2, q=CHUNK),
                                             gn[:, 0:1], None, ALU.mult)
                    last.then_inc(tp_free.sem, 1)

            def y_out(b, u):
                yb = y_bank(u)
                dve.wait_ge(y_half.sem, y_half.at(b, PV_UNITS.index(u) + 1))
                if u < MEM_UNITS:
                    t, a = min(MEM_UNIT[u - 1], MEM_UNIT[u])
                    for hp in range(2):
                        h = slice(64 * hp, 64 * hp + 64)
                        last = dve.tensor_tensor(y[h, a, t * P:(t + 2) * P], yb[0:64, hp * 256:(hp + 1) * 256],
                                                 y_lows[h, 0:256], ALU.add)
                else:
                    c, g = (u - MEM_UNITS) // 2, (u - MEM_UNITS) % 2
                    h = slice(64 * g, 64 * g + 64)
                    last = dve.tensor_tensor(y[h, 2:10, c * CHUNK:(c + 1) * CHUNK],
                                             yb[0:64, :].rearrange("p (j q) -> p j q", q=CHUNK),
                                             y_lows[h, :].rearrange("p (j q) -> p j q", q=CHUNK), ALU.add)
                last.then_inc(y_free.sem, 1)

            def place(b, n, t):
                q = 4 * n + t
                scored = stage(q, 0)
                for u in scored:
                    if u == MEM_UNITS:
                        dve.wait_ge(bias_set.sem, 4)
                    dve.wait_ge(sc_full.sem, sc_full.at(b, u + 1))
                for u in stage(q, 1):
                    denominators(b, u)
                if scored and stage(q, 1):
                    scores(b, scored.pop())
                for u in outputs_of(q - 3):
                    y_out(b, u)
                tp_event(b, n, t)
                if t == 0 and n + LEAD not in POOL_LO:
                    lo_of_chunk(n + LEAD, raw_chunk(n + LEAD), w_hi.at(b, n + LEAD + 1))
                for u in scored:
                    scores(b, u)
                accumulator(b, n, t)
                if (n, t) in SILU:
                    k, i = SILU[n, t]
                    dve.wait_ge(g_th.sem, g_th.at(b, k + 1))
                    dve.scalar_tensor_tensor(out=gate[:, k, :], in0=u_tok[:, i, :] if k >= 2 else tmp[:, i, :],
                                             scalar=1.0, in1=gate[:, k, :], op0=ALU.add,
                                             op1=ALU.mult).then_inc(g_done.sem, 1)

            def accumulator(b, n, t):
                if n in G_ENDS and t >= 4 - G_ENDS[n][1]:
                    k0, kn = G_ENDS[n]
                    i = t - (4 - kn)
                    dve.wait_ge(acc_done.sem, acc_done.at(b, 12 + k0 + i + 1))
                    dve.tensor_tensor(gate[:, k0 + i, :], acc[i][:], rbc[:], ALU.mult).then_inc(g_raw.sem, 1)
                if n in O_ENDS:
                    o = O_ENDS[n]
                    if t == 0:
                        dve.wait_ge(res_full.sem, res_full.at(b, 16 * (o + 1)))
                    dve.wait_ge(acc_done.sem, acc_done.at(b, 22 + 4 * o + t + 1))
                    dve.tensor_tensor(res[:, t, :], acc[t][:], res[:, t, :], ALU.add).then_inc(o_done.sem, 1)

            def head_norms(b, n, half_):
                for s, e in enumerate(A_ENDS):
                    if n in (e + 1, e + 2):
                        t = 2 * (n - e - 1) + half_
                        head_squares(t, 8, u_sq.at(b, 4 * s + t + 1), u_ss.at(b, 4 * s + t + 1))
                        if s == 0:
                            dve.wait_ge(v_hi.sem, v_hi.at(b, t + 1))
                            dve.tensor_tensor(vO[:, t, :, HD:], heads(u_tok[:, t, P:2 * P]),
                                              vO[:, t, :, 0:HD].bitcast(F32), ALU.subtract).then_inc(v_lo.sem, 1)
                    if n in (e + 2, e + 3):
                        t = 2 * (n - e - 2) + half_
                        dve.wait_ge(u_r.sem, u_r.at(b, 4 * s + t + 1))
                        if s == 0:
                            scale_heads(t, 0, 2)
                            scale_heads(t, 4, 8).then_inc(u_n.sem, 1)
                        else:
                            scale_heads(t, 0, 8).then_inc(u_n.sem, 1)

            with dve.Fori(0, BLOCKS) as b:
                for n in range(STEPS):
                    if n == R_DIAG:
                        dve.wait_ge(x_r.sem, x_r.at(b, TILES))
                        for t in range(TILES):
                            last = dve.tensor_scalar(tmp[:, 0, t * P:(t + 1) * P], ident[:], xr[:, t:t + 1], None,
                                                     ALU.mult)
                        last.then_inc(r_diag.sem, 1)
                    place(b, n, 0)
                    place(b, n, 1)
                    head_norms(b, n, 0)
                    if n == V_EVEN:
                        dve.wait_ge(v_lo.sem, v_lo.at(b, TILES))
                        dve.wait_ge(halo.sem, halo.at(b, 0))
                        dve.tensor_copy(vE[0:64, 0:TILES].rearrange("p t a d -> p (t a d)"),
                                        vO[0:64].rearrange("p t a d -> p (t a d)").bitcast(F32))
                        dve.tensor_copy(vE[64:128, 1:].rearrange("p t a d -> p (t a d)"),
                                        vO[64:128].rearrange("p t a d -> p (t a d)").bitcast(F32)).then_inc(v_even.sem, 1)
                    if n in X_SQUARE:
                        k = X_SQUARE[n]
                        x_mean(k, x_sq.at(b, k + 1))
                    if n in X_SPLIT:
                        k = X_SPLIT[n]
                        x_lo_part(k, slice(0, 512), xraw[:, k % 2, :], 0, x_hi.at(b, k + 1))
                    place(b, n, 2)
                    place(b, n, 3)
                    head_norms(b, n, 1)
                    if O_0 - 2 <= n < STEPS - 2:
                        i = n + 2 - O_0
                        dve.wait_ge(y_hi.sem, y_hi.at(b, i + 1))
                        dve.tensor_tensor(ys[:, i % YRING, 1, :], y[:, i % YT, :], ys[:, i % YRING, 0, :].bitcast(F32),
                                          ALU.subtract).then_inc(y_lo.sem, 1)
                    if n == HALO:
                        dve.wait_ge(y_full.sem, y_full.at(b, len(PV_UNITS)))
                        dve.tensor_copy(bias[:, 2], bias[:, 0])
                        dve.tensor_copy(vE[64:128, 0], vE[64:128, TILES].bitcast(F32))
                        dve.tensor_copy(kTe[:, 0, 1, :], kTe[:, TILES, 1, :]).then_inc(halo.sem, 1)

        @block.tensor
        def _(pe):
            for c in range(PRO_CHUNKS):
                pe.wait_ge(w_lo.sem, c + 1)
                if c < 4:
                    pe.wait_ge(x_lo.sem, 2 * c + 2)
                for t in range(2):
                    bank = acc[t if c < 4 else 2 + t][:, 0:256]
                    for kk in range(2):
                        k = 2 * (c % 4) + kk
                        for i, (a, w) in enumerate(PASSES):
                            last = pe.matmul(bank, xnT[:, a, k, t * P:(t + 1) * P],
                                             ws[:, c % WRING, w, kk * 256:(kk + 1) * 256],
                                             start=(k == 0 and i == 0), stop=(k == KT - 1 and i == 2))
                    if c % 4 == 3:
                        last.then_inc(acc_done.sem, 1)
                if c % 4 < 3:
                    last.then_inc(step_done.sem, 1)
            pe.wait_ge(const.sem, 64)
            for t in range(2):
                pe.wait_ge(u_n.sem, t + 1)
                for j in range(2):
                    last = pe.transpose(turn[t][:, j * P:(j + 1) * P], u_tok[:, t, j * P:(j + 1) * P], ident[:])
                last.then_inc(tp_full.sem, 1)

            def qk(b, u):
                if u > 0:
                    pe.wait_ge(sc_neg.sem, sc_neg.at(b, u))
                if u == MEM_UNITS:
                    pe.wait_ge(halo.sem, halo.at(b, 0))
                if u == 0:
                    pe.wait_ge(mk_both.sem, 2)
                if u < MEM_UNITS:
                    t, a = MEM_UNIT[u]
                    pe.wait_ge(tp_free.sem, tp_free.at(b, TP_OF["q", 0, t] + 1))
                    for hp in range(2):
                        head = 2 * hp + a
                        for part in range(2):
                            last = pe.matmul(sc[:, hp * 256:(hp + 1) * 256], mq[:, head, t * P:(t + 1) * P],
                                             mk[:, head, part, :], start=(part == 0), stop=(part == 1))
                else:
                    c, g = (u - MEM_UNITS) // 2, (u - MEM_UNITS) % 2
                    t = c // 2
                    pe.wait_ge(tp_free.sem, tp_free.at(b, TP_OF["q", 2, t] + 1))
                    h = slice(64 * g, 64 * g + 64)
                    keys = kTo[h, t, :] if c % 2 else kTe[h, t, :, :].rearrange("p a b -> p (a b)")
                    for p in range(4):
                        last = pe.matmul(sc[:, p * P:(p + 1) * P],
                                         qT[h, c, 2 * p:2 * p + 2, :].rearrange("p a b -> p (a b)"), keys,
                                         start=True, stop=True)
                last.then_inc(sc_full.sem, 1)

            def p_transposes(b, u, bank):
                pe.wait_ge(p_norm.sem, p_norm.at(b, u + 1))
                for j in range(4):
                    i = (j % 2) * 2 + j // 2 if u < MEM_UNITS else j
                    last = pe.transpose(bank[:, j * P:(j + 1) * P], ps[:, u % 3, i * P:(i + 1) * P], ident[:])
                return last

            def pv(b, u):
                pe.wait_ge(tp_free.sem, tp_free.at(b, TP_OF["p", u, 0] + 1))
                yb = y_bank(u)
                free = bank_read(b, Y_TURNS[PV_UNITS.index(u)])
                pe.wait_ge(free[0].sem, free[1])
                if u < MEM_UNITS:
                    a = MEM_UNIT[u][1]
                    r = min(PT_SLOT[u - 1], PT_SLOT[u])
                    for hp in range(2):
                        for kt in range(2):
                            for p in range(2):
                                last = pe.matmul(
                                    yb[:, hp * 256:(hp + 1) * 256].rearrange("d (t q) -> d t q", t=2),
                                    mv[:, kt, 2 * a + hp, :],
                                    pT[:, r:r + 2, p, (2 * kt + hp) * P:(2 * kt + hp + 1) * P],
                                    start=(kt == 0 and p == 0), stop=(kt == 1 and p == 1))
                else:
                    c, g = (u - MEM_UNITS) // 2, (u - MEM_UNITS) % 2
                    pe.wait_ge(v_even.sem, v_even.at(b, 1))
                    for p in range(2):
                        last = pe.matmul(yb[:], (vO if c % 2 else vE)[:, c // 2, g, :], pT[:, PT_SLOT[u], p, :],
                                         start=(p == 0), stop=(p == 1))
                last.then_inc(y_full.sem, 1)

            def tp_event(b, n, place):
                key = (n, place)
                if key not in TP_INDEX:
                    return
                kind, i, h = TP_AT[key]
                bank = tp_bank(key)
                free = bank_read(b, TURN_OF[4 * n + place, "tp"])
                pe.wait_ge(free[0].sem, free[1])
                if kind == "r":
                    pe.wait_ge(r_diag.sem, r_diag.at(b, 1))
                    pe.matmul(bank[:], ones[:], tmp[:, 0, :], start=True, stop=True).then_inc(tp_full.sem, 1)
                    return
                if kind == "p":
                    p_transposes(b, i, bank).then_inc(tp_full.sem, 1)
                    return
                s, t = i, h
                pe.wait_ge(u_n.sem, u_n.at(b, 4 * s + t + 1))
                cols = (0, 2, 3) if s == 0 else (0, 1, 2, 3)
                for j, cblk in enumerate(cols):
                    last = pe.transpose(bank[:, j * P:(j + 1) * P], u_tok[:, t, cblk * P:(cblk + 1) * P], ident[:])
                last.then_inc(tp_full.sem, 1)

            def group(b, n, t):
                ring = n % WRING
                if n < G_0:
                    k, K = n % 8, KT
                    return [(xnT[:, a, k, t * P:(t + 1) * P], ws[:, ring, w, :]) for a, w in PASSES], k == 0, k == K - 1
                if n < G_1:
                    m = n - G_0
                    kk, g = divmod(t, 2)
                    return [(ws[:, ring, w, kk * 256 + g * P:kk * 256 + (g + 1) * P], xnT[:, a, 2 * m + kk, :])
                            for w, a in PASSES], m + kk == 0, m + kk == 4
                if n < O_0:
                    k = (n - G_1) % 8
                    return [(ws[:, ring, w, t * P:(t + 1) * P], xnT[:, a, k, :]) for w, a in PASSES], k == 0, k == 7
                k = (n - O_0) % YT
                yr = (n - O_0) % YRING
                return [(ys[:, yr, a, t * P:(t + 1) * P], ws[:, ring, w, :]) for a, w in PASSES], k == 0, k == YT - 1

            with pe.Fori(0, BLOCKS) as b:
                for n in range(STEPS):
                    split = lo_done(b, n)
                    pe.wait_ge(split[0].sem, split[1])
                    if n >= O_0:
                        pe.wait_ge(y_lo.sem, y_lo.at(b, n - O_0 + 1))
                    if n < KT:
                        pe.wait_ge(x_lo.sem, x_lo.at(b, n + 1 - KT))
                    for t in range(4):
                        for u in outputs_of(4 * n + t - 2):
                            pv(b, u)
                        for u in stage(4 * n + t, 0):
                            qk(b, u)
                        tp_event(b, n, t)
                        ops, first, final = group(b, n, t)
                        if first:
                            who, how_many = bank_free(n, t)
                            cnt = {"o_done": o_done, "u_raw": u_raw, "g_raw": g_raw}[who]
                            pe.wait_ge(cnt.sem, cnt.at(b, how_many))
                            if (n, t) == (A_KV, 2):
                                pe.wait_ge(v_lo.sem, v_lo.at(b, 0))
                        for i, (lhs, rhs) in enumerate(ops):
                            last = pe.matmul(acc[t % 2 if G_0 <= n < G_1 else t][:], lhs, rhs, start=(first and i == 0),
                                             stop=(final and i == len(ops) - 1))
                        if final:
                            last.then_inc(acc_done.sem, 1)
                    if not final:
                        last.then_inc(step_done.sem, 1)


def head_columns():
    import numpy as np

    d = np.arange(HD)
    mem_cols = [N_HEADS * HD + h * HD + d for h in (0, 2, 1, 3)]
    win_cols = [h * HD + d for j in range(PAIRS) for h in (j, PAIRS + j)]
    return np.concatenate(mem_cols), np.concatenate(win_cols)


def alibi_constants():
    import numpy as np

    slopes = np.float32(2.0) ** (np.float32(-8.0) * np.arange(1, N_HEADS + 1, dtype=np.float32) / np.float32(N_HEADS))
    dist = np.abs(np.arange(CHUNK)[:, None] - np.arange(2 * CHUNK)[None, :] + CHUNK).astype(np.float32)
    even = np.concatenate([dist[:, CHUNK:], dist[:, :CHUNK]], axis=1)
    by_pair = np.repeat(-slopes.reshape(PAIRS, 2).T, CHUNK, axis=0)
    return np.concatenate([by_pair, np.tile(even, (2, 1)), np.tile(dist, (2, 1))], axis=1)


def kernel(**inputs):
    import numpy as np
    import concourse.bacc as bacc
    from concourse.bass_utils import run_bass_kernel_spmd

    f32 = np.float32
    x = np.ascontiguousarray(inputs["x"]).reshape(SEQ, D_MODEL)
    mem = np.ascontiguousarray(inputs["mem"]).reshape(N_MEM, D_MODEL)
    w_in = np.asarray(inputs["a_w_in"])[0]
    w_out = np.asarray(inputs["w_out"])[0]
    mem_cols, win_cols = head_columns()
    kv0 = N_HEADS * HD
    mq0 = kv0 + 2 * KV_HEADS * HD
    g0 = mq0 + MEM_HEADS * HD
    w_kv = np.asarray(inputs["mem_w_kv"])
    gate_cols = g0 + np.concatenate([mem_cols, win_cols])

    def chunks(w):
        k, n = w.shape
        return w.reshape(k // P, P, n).transpose(1, 0, 2).reshape(P, -1)

    slices = [w_in[:, kv0:g0], w_in[:, win_cols[:512]], w_in[:, win_cols[512:]],
              w_in[:, gate_cols[256:768]], w_in[:, gate_cols[768:]]]
    w_rows = w_out[np.concatenate([mem_cols, win_cols])]
    gains = [inputs["a_q_norm_g"][0], inputs["mem_q_norm_g"][0], inputs["a_k_norm_g"][0], inputs["mem_k_norm_g"]]
    arrays = {
        "x": np.concatenate([x, np.zeros((BLOCK, D_MODEL), f32)]),
        "xT": np.concatenate([x.reshape(BLOCKS, BLOCK, KT, P).transpose(0, 3, 2, 1).reshape(BLOCKS, P, -1),
                              np.zeros((1, P, KT * BLOCK), f32)]),
        "mem": mem,
        "memT": mem.reshape(N_MEM, KT, P).transpose(2, 1, 0).reshape(P, -1),
        "w_in": np.stack([chunks(w) for w in slices]),
        "w_gate0": chunks(w_in[:, gate_cols[:256]]),
        "w_out": np.stack([chunks(w_rows[:, :512]), chunks(w_rows[:, 512:])]),
        "w_kv": np.concatenate([chunks(w_kv[:, :256]), chunks(w_kv[:, mem_cols - kv0 + 256])], axis=1),
        "norm_gains": np.concatenate([np.asarray(inputs[g]).reshape(KT, P).T for g in ("norm_g", "mem_norm_g")], axis=1),
        "gains": np.stack([np.tile(np.asarray(g), 2) for g in gains], axis=1),
        "sink": np.repeat(np.asarray(inputs["a_sink"])[0].reshape(PAIRS, 2).T, CHUNK, axis=0),
        "ident": np.eye(P, dtype=f32),
        "alibi": alibi_constants(),
    }
    nc = bacc.Bacc("TRN2", target_bir_lowering=False, num_devices=1)
    feeds, args = {}, []
    for name, a in arrays.items():
        a = np.ascontiguousarray(a)
        feeds[f"in_{name}"] = a
        args.append(nc.dram_tensor(f"in_{name}", a.shape, F32, kind="ExternalInput").ap())
    args.append(nc.dram_tensor("out_0", (SEQ, D_MODEL), F32, kind="ExternalOutput").ap())
    encoder_layer(nc, *args)
    r = run_bass_kernel_spmd(nc, [feeds], core_ids=[0])
    return r.results[0]["out_0"].reshape(1, SEQ, D_MODEL)
```
